# Optimizing a Trainium2 kernel written in Bass

```python
import math
import jax, jax.numpy as jnp
from jax import lax
import numpy as np

D_MODEL = 1024
BATCH = 1
SEQ = 512
DEPTH = 2

HEAD_DIM = 64
SWA_Q_HEADS = 8
SWA_KV_HEADS = 2
SWA_GROUP = SWA_Q_HEADS // SWA_KV_HEADS
SWA_WINDOW = 128
MOBA_HEADS = 8
MOBA_BLOCK = 256
MOBA_TOPK = 3
MOBA_Q_CHUNK = 128
HGRN_HEADS = 8
HGRN_DK = D_MODEL // HGRN_HEADS
HGRN_DV = D_MODEL // HGRN_HEADS
HGRN_WIDTH = HGRN_HEADS * HGRN_DK
HGRN_CHUNK = 64
D_FF = 2816
N_EVEN = (DEPTH + 1) // 2
N_ODD = DEPTH // 2
DEEPNORM_ALPHA = (2 * DEPTH) ** 0.25
DEEPNORM_BETA = (8 * DEPTH) ** -0.25
FFN_RES_WEIGHT = 0.5
LN_EPS = 1e-5
RMS_EPS = 1e-6
ATTN_SCALE = HEAD_DIM ** -0.5
SWA_Q_W = SWA_Q_HEADS * HEAD_DIM
SWA_KV_W = SWA_KV_HEADS * HEAD_DIM
MOBA_W = MOBA_HEADS * HEAD_DIM
EVEN_SPLITS = (SWA_Q_W, SWA_Q_W + SWA_KV_W, SWA_Q_W + 2 * SWA_KV_W,
               SWA_Q_W + 2 * SWA_KV_W + MOBA_W, SWA_Q_W + 2 * SWA_KV_W + 2 * MOBA_W)
EVEN_IN_WIDTH = SWA_Q_W + 2 * SWA_KV_W + 3 * MOBA_W
EVEN_OUT_WIDTH = SWA_Q_W + MOBA_W

kernel_name = "hybrid_swa_moba_hgrn2_deepnorm_macaron"

def layer_norm(x, g, b):
    xf = x.astype(jnp.float32)
    mu = jnp.mean(xf, axis=-1, keepdims=True)
    var = jnp.mean(jnp.square(xf - mu), axis=-1, keepdims=True)
    return ((xf - mu) * lax.rsqrt(var + LN_EPS) * g.astype(jnp.float32) + b.astype(jnp.float32)).astype(x.dtype)

def rms_norm(x, g):
    xf = x.astype(jnp.float32)
    return xf * lax.rsqrt(jnp.mean(jnp.square(xf), axis=-1, keepdims=True) + RMS_EPS) * g.astype(jnp.float32)

def swiglu(x, w1, w3, w2):
    return (jax.nn.silu(x @ w1) * (x @ w3)) @ w2

def alibi_slopes(n):
    return 2.0 ** (-8.0 * jnp.arange(1, n + 1, dtype=jnp.float32) / n)

def swa_sink_attention(q, k, v, sinks, slopes):
    B, S = q.shape[0], q.shape[1]
    W = SWA_WINDOW
    nb = S // W
    f32 = jnp.float32
    qb = q.reshape(B, nb, W, SWA_KV_HEADS, SWA_GROUP, HEAD_DIM).astype(f32)
    kb = k.reshape(B, nb, W, SWA_KV_HEADS, HEAD_DIM).astype(f32)
    vb = v.reshape(B, nb, W, SWA_KV_HEADS, HEAD_DIM).astype(f32)
    pad = ((0, 0), (1, 0), (0, 0), (0, 0), (0, 0))
    kk = jnp.concatenate([jnp.pad(kb, pad)[:, :-1], kb], axis=2)
    vv = jnp.concatenate([jnp.pad(vb, pad)[:, :-1], vb], axis=2)
    scores = jnp.einsum('bnqhgd,bnkhd->bnhgqk', qb, kk) * ATTN_SCALE
    qi = jnp.arange(W)[:, None]
    kj = jnp.arange(2 * W)[None, :]
    dist = qi + W - kj
    band = (dist >= 0) & (dist < W)
    not_before_start = (jnp.arange(nb)[:, None, None] > 0) | (kj[None] >= W)
    valid = band[None] & not_before_start
    logits = scores - slopes.astype(f32)[:, :, None, None] * dist.astype(f32)
    logits = jnp.where(valid[None, :, None, None], logits, -jnp.inf)
    sink = sinks.astype(f32)[None, None, :, :, None, None]
    m = jnp.maximum(jnp.max(logits, axis=-1, keepdims=True), sink)
    p = jnp.exp(logits - m)
    denom = jnp.sum(p, axis=-1, keepdims=True) + jnp.exp(sink - m)
    o = jnp.einsum('bnhgqk,bnkhd->bnqhgd', p / denom, vv)
    return o.reshape(B, S, SWA_KV_HEADS * SWA_GROUP * HEAD_DIM)

def moba_attention(q, k, v, slopes):
    B, S, H, Dh = q.shape
    f32 = jnp.float32
    Sp = -(-S // MOBA_BLOCK) * MOBA_BLOCK
    pad = ((0, 0), (0, Sp - S), (0, 0), (0, 0))
    q = jnp.pad(q, pad)
    k = jnp.pad(k, pad)
    v = jnp.pad(v, pad)
    nb = Sp // MOBA_BLOCK
    nq = Sp // MOBA_Q_CHUNK
    Q = MOBA_Q_CHUNK
    K = min(MOBA_TOPK, nb)
    qh = jnp.transpose(q, (0, 2, 1, 3)).astype(f32)
    kb = jnp.transpose(k, (0, 2, 1, 3)).astype(f32).reshape(B, H, nb, MOBA_BLOCK, Dh)
    vb = jnp.transpose(v, (0, 2, 1, 3)).astype(f32).reshape(B, H, nb, MOBA_BLOCK, Dh)
    kmean = jnp.mean(kb, axis=3)
    q_chunks = qh.reshape(B, H, nq, Q, Dh).transpose(2, 0, 1, 3, 4)
    bidx = jnp.arange(B)[:, None, None, None]
    hidx = jnp.arange(H)[None, :, None, None]
    blk_pos = jnp.arange(MOBA_BLOCK)
    slope = slopes.astype(f32)[None, :, None, None]

    def one_chunk(args):
        c, qc = args
        t = c * Q + jnp.arange(Q)
        own = (c * Q) // MOBA_BLOCK
        gate = jnp.einsum('bhqd,bhnd->bhqn', qc, kmean)
        gate = jnp.where(jnp.arange(nb) < own, gate, -jnp.inf)
        top_val, top_idx = lax.top_k(gate, K)
        sel_ok = top_val > -jnp.inf
        kg = kb[bidx, hidx, top_idx]
        vg = vb[bidx, hidx, top_idx]
        s_sel = jnp.einsum('bhqd,bhqjkd->bhqjk', qc, kg) * ATTN_SCALE
        pos_sel = top_idx[..., None] * MOBA_BLOCK + blk_pos
        d_sel = (t[None, None, :, None, None] - pos_sel).astype(f32)
        s_sel = jnp.where(sel_ok[..., None], s_sel - slope[..., None] * d_sel, -jnp.inf)
        k_own = lax.dynamic_index_in_dim(kb, own, axis=2, keepdims=False)
        v_own = lax.dynamic_index_in_dim(vb, own, axis=2, keepdims=False)
        s_own = jnp.einsum('bhqd,bhkd->bhqk', qc, k_own) * ATTN_SCALE
        d_own = t[:, None] - (own * MOBA_BLOCK + blk_pos)[None, :]
        s_own = jnp.where(d_own >= 0, s_own - slope * d_own.astype(f32), -jnp.inf)
        n_sel = K * MOBA_BLOCK
        logits = jnp.concatenate([s_sel.reshape(B, H, Q, n_sel), s_own], axis=-1)
        p = jax.nn.softmax(logits, axis=-1)
        p_sel = p[..., :n_sel].reshape(B, H, Q, K, MOBA_BLOCK)
        p_own = p[..., n_sel:]
        return (jnp.einsum('bhqjk,bhqjkd->bhqd', p_sel, vg)
                + jnp.einsum('bhqk,bhkd->bhqd', p_own, v_own))

    out = lax.map(one_chunk, (jnp.arange(nq), q_chunks))
    out = out.transpose(1, 0, 3, 2, 4).reshape(B, Sp, H * Dh)
    return out[:, :S]

def hybrid_attention(x, w_in, sinks, w_out):
    B, S, _ = x.shape
    proj = x @ w_in
    qa, ka, va, qb, kb, vb = jnp.split(proj, EVEN_SPLITS, axis=-1)
    slopes = alibi_slopes(SWA_Q_HEADS + MOBA_HEADS)
    oa = swa_sink_attention(
        qa.reshape(B, S, SWA_KV_HEADS, SWA_GROUP, HEAD_DIM),
        ka.reshape(B, S, SWA_KV_HEADS, HEAD_DIM),
        va.reshape(B, S, SWA_KV_HEADS, HEAD_DIM),
        sinks.reshape(SWA_KV_HEADS, SWA_GROUP),
        slopes[:SWA_Q_HEADS].reshape(SWA_KV_HEADS, SWA_GROUP))
    ob = moba_attention(
        qb.reshape(B, S, MOBA_HEADS, HEAD_DIM),
        kb.reshape(B, S, MOBA_HEADS, HEAD_DIM),
        vb.reshape(B, S, MOBA_HEADS, HEAD_DIM),
        slopes[SWA_Q_HEADS:])
    o = jnp.concatenate([oa, ob], axis=-1).astype(x.dtype)
    return o @ w_out

def hgrn2(x, w_in, norm_g, w_out, lb):
    B, S, _ = x.shape
    f32 = jnp.float32
    proj = x @ w_in
    q, f, i, g = jnp.split(proj, 4, axis=-1)
    ff = f.astype(f32)
    lbf = lb.astype(f32)
    log_f = jnp.logaddexp(jnp.log(lbf), jnp.log1p(-lbf) + jax.nn.log_sigmoid(ff))
    k = (1.0 - lbf) * jax.nn.sigmoid(-ff)
    q = jax.nn.silu(q.astype(f32))
    v = i.astype(f32)
    nc = S // HGRN_CHUNK
    C = HGRN_CHUNK

    def to_chunks(a, dim):
        return a.reshape(B, nc, C, HGRN_HEADS, dim).transpose(1, 0, 3, 2, 4)

    qs, ks, gs = to_chunks(q, HGRN_DK), to_chunks(k, HGRN_DK), to_chunks(log_f, HGRN_DK)
    vs = to_chunks(v, HGRN_DV)
    causal = jnp.tril(jnp.ones((C, C), dtype=bool))

    def step(state, inp):
        qc, kc, vc, gc = inp
        b = jnp.cumsum(gc, axis=2)
        o_inter = jnp.einsum('bhtk,bhkv->bhtv', qc * jnp.exp(b), state)
        diff = b[:, :, :, None, :] - b[:, :, None, :, :]
        decay = jnp.exp(jnp.where(causal[:, :, None], diff, -jnp.inf))
        a = jnp.einsum('bhtk,bhsk,bhtsk->bhts', qc, kc, decay)
        o_intra = jnp.einsum('bhts,bhsv->bhtv', a, vc)
        b_last = b[:, :, -1:, :]
        new_state = (jnp.exp(b_last[:, :, 0, :])[..., None] * state
                     + jnp.einsum('bhsk,bhsv->bhkv', kc * jnp.exp(b_last - b), vc))
        return new_state, o_inter + o_intra

    state0 = jnp.zeros((B, HGRN_HEADS, HGRN_DK, HGRN_DV), f32)
    _, o = lax.scan(step, state0, (qs, ks, vs, gs))
    o = o.transpose(1, 0, 3, 2, 4).reshape(B, S, HGRN_HEADS, HGRN_DV)
    o = rms_norm(o, norm_g).reshape(B, S, HGRN_WIDTH) * jax.nn.silu(g.astype(f32))
    return o.astype(x.dtype) @ w_out

def setup_inputs(seed: int = 0) -> dict:
    key = jax.random.key(seed)
    ks = jax.random.split(key, 13)
    f32 = jnp.float32

    def nrm(k, shape, scale):
        return jax.random.normal(k, shape, f32) * scale

    return {
        "x": nrm(ks[0], (BATCH, SEQ, D_MODEL), 1.0),
        "ffn_w1": nrm(ks[1], (DEPTH, 2, D_MODEL, D_FF), D_MODEL ** -0.5),
        "ffn_w3": nrm(ks[2], (DEPTH, 2, D_MODEL, D_FF), D_MODEL ** -0.5),
        "ffn_w2": nrm(ks[3], (DEPTH, 2, D_FF, D_MODEL), D_FF ** -0.5 * DEEPNORM_BETA),
        "ln_g": 1.0 + nrm(ks[4], (DEPTH, 3, D_MODEL), 0.02),
        "ln_b": nrm(ks[5], (DEPTH, 3, D_MODEL), 0.02),
        "attn_w_in": nrm(ks[6], (N_EVEN, D_MODEL, EVEN_IN_WIDTH), D_MODEL ** -0.5),
        "attn_sinks": nrm(ks[7], (N_EVEN, SWA_Q_HEADS), 1.0),
        "attn_w_out": nrm(ks[8], (N_EVEN, EVEN_OUT_WIDTH, D_MODEL), EVEN_OUT_WIDTH ** -0.5 * DEEPNORM_BETA),
        "hgrn_w_in": nrm(ks[9], (N_ODD, D_MODEL, 4 * HGRN_WIDTH), D_MODEL ** -0.5),
        "hgrn_norm_g": 1.0 + nrm(ks[10], (N_ODD, HGRN_DV), 0.02),
        "hgrn_w_out": nrm(ks[11], (N_ODD, HGRN_WIDTH, D_MODEL), HGRN_WIDTH ** -0.5 * DEEPNORM_BETA),
        "hgrn_lower_bounds": nrm(ks[12], (DEPTH, HGRN_WIDTH), 0.1),
    }

def reference(x, ffn_w1, ffn_w3, ffn_w2, ln_g, ln_b, attn_w_in, attn_sinks, attn_w_out,
              hgrn_w_in, hgrn_norm_g, hgrn_w_out, hgrn_lower_bounds):
    lbs = jnp.cumsum(jax.nn.softmax(hgrn_lower_bounds.astype(jnp.float32), axis=0), axis=0)
    lbs = lbs - lbs[0:1]
    for l in range(DEPTH):
        j = l // 2
        h = swiglu(x, ffn_w1[l, 0], ffn_w3[l, 0], ffn_w2[l, 0])
        x = layer_norm(DEEPNORM_ALPHA * x + FFN_RES_WEIGHT * h, ln_g[l, 0], ln_b[l, 0])
        if l % 2 == 0:
            h = hybrid_attention(x, attn_w_in[j], attn_sinks[j], attn_w_out[j])
        else:
            h = hgrn2(x, hgrn_w_in[j], hgrn_norm_g[j], hgrn_w_out[j], lbs[l])
        x = layer_norm(DEEPNORM_ALPHA * x + h, ln_g[l, 1], ln_b[l, 1])
        h = swiglu(x, ffn_w1[l, 1], ffn_w3[l, 1], ffn_w2[l, 1])
        x = layer_norm(DEEPNORM_ALPHA * x + FFN_RES_WEIGHT * h, ln_g[l, 2], ln_b[l, 2])
    return x


_drawn_inputs = setup_inputs


def setup_inputs(seed=0):
    import zlib

    import numpy as np

    out = dict(_drawn_inputs(seed))
    spreads = {}
    factors = {'attn_sinks': 8.0, 'hgrn_norm_g': 23.349, 'hgrn_lower_bounds': 8.0}
    for name, (base, spread) in spreads.items():
        noise = np.random.default_rng([zlib.crc32(name.encode()), seed]).standard_normal(out[name].shape)
        drawn = base * np.exp(spread * noise) if base else spread * noise
        out[name] = __import__('jax').numpy.asarray(drawn.astype(out[name].dtype))
    for name, factor in factors.items():
        out[name] = (out[name] * factor).astype(out[name].dtype)
    return out
```

```python
import numpy as np
import concourse.bass as bass
from concourse import mybir
from contextlib import ExitStack

F32 = mybir.dt.float32
F32R = mybir.dt.float32r
I32 = mybir.dt.int32
ALU = mybir.AluOpType
ACT = mybir.ActivationFunctionType
AX = mybir.AxisListType

P = 128
D = 1024
T = 512
DFF = 2816
NT = T // P
DC = D // P
GW = 256
NG = DFF // GW
SLAB = 2048
RING = 3
HALF = D // 2
ALPHA = 4.0 ** 0.25
LN_EPS = 1e-5 / (ALPHA * ALPHA)
RMS_EPS = 1e-6
LEVELS = [1, 2, 4, 8, 16, 32, 64]
MASK_STEPS = 1 + 2 * len(LEVELS)
TABLE_STEPS = 4 * 3 + 4 * 2
BLOCKS = 18
ARENA = 14464
FREE_AT_START = 4
HD = 64
SCALE = HD ** -0.5
SLOPES = [2.0 ** (-8.0 * (i + 1) / 16) for i in range(16)]
WINDOW = 128
FAR = 1.0e30
CH = 128

PHASES = [("ffn", (0, 0), (0, 0), 0.5), ("attn", 0, (0, 1), 1.0), ("ffn", (0, 1), (0, 2), 0.5),
          ("ffn", (1, 0), (1, 0), 0.5), ("hgrn", 0, (1, 1), 1.0), ("ffn", (1, 1), (1, 2), 0.5)]
SIZES = {"ffn": (3 * NG, NG), "attn": (13, 4), "hgrn": (20, 4)}


def layout(phases):
    out, s, k = [], 0, 0
    for ph in phases:
        out.append((s, k))
        s += SIZES[ph[0]][0]
        k += SIZES[ph[0]][1]
    return out, s


FQGV = {"f": 1, "q": 0, "g": 3, "v": 2}


def mixer_schedule(kind):
    if kind == "attn":
        projections = [["kv", "q"], ["q"], ["kb", "vb", "q"], ["kb", "vb", "q"]]
    else:
        projections = [list(FQGV)] * 4
    slabs = [(name, 0) for name in projections[0]]
    steps = [("quarter", s, c) for s in range(len(slabs)) for c in range(4)]
    unit = 0
    for g in range(4):
        names = [(name, g + 1) for name in projections[g + 1]] if g < 3 else []
        if g:
            names.append(("down", g - 1))
        fill = [("quarter", len(slabs) + s, c) for s in range(len(names)) for c in range(4)]
        slabs += names
        if kind == "attn":
            own = [("scores", unit)]
            n = 4 if g < 2 else 8
            for u in range(unit, unit + n):
                own += [("turn_probs", u)] + ([("scores", u + 1)] if u + 1 < unit + n else []) + [None, ("values", u), None]
            unit += n
            own = own[:-1] + [None, ("turn_out", g)]
        else:
            own = [("level", g, m) for m in range(8)] + [("turn_keys", g), ("updates", g), ("outputs", g)]
            own = [x for step in own for x in (step, None)] + [None, ("turn_out", g)]
        gaps, put = own.count(None), 0
        seen = 0
        for step in own:
            if step is not None:
                steps.append(step)
                continue
            seen += 1
            upto_ = len(fill) * seen // gaps
            steps += fill[put:upto_]
            put = upto_
    slabs.append(("down", 3))
    return slabs, steps


SWA_UNIT = ([(0, [0]), (1, [0, 1]), (2, [1, 2]), (3, [2, 3])], P)
MOBA_UNITS = [([(0, [0]), (2, [0, 1, 2]), (1, [0, 1])], 0), ([(3, [0, 1, 2, 3])], 0)]


def attention_unit(u):
    if u < 8:
        return u, SWA_UNIT[0], SWA_UNIT[1], True
    return 8 + (u - 8) // 2, *MOBA_UNITS[u % 2], u % 2 == 1


def decay_at(m):
    return 2 * T - 4 * T // m


def two_bank_units(u):
    return min(u, 8) + (max(u - 8, 0) + 1) // 2


def build_trunk(nc, x_in, w1, w3, w2, ln_g, ln_b, aw_in, sinks, aw_out, hw_in, hnorm, hw_out, lbs_in, out,
                phases=None):
    phases = PHASES if phases is None else phases
    bases, n_slabs = layout(phases)
    ffn_index = [sum(p[0] == "ffn" for p in phases[:n]) for n in range(len(phases))]
    last_phase = len(phases) - 1

    with ExitStack() as ctx:
        def sb(name, shape, dt=F32):
            return ctx.enter_context(nc.sbuf_tensor(name, shape, dt))

        def sem(name):
            return ctx.enter_context(nc.semaphore(name))

        raw = sb("raw", [P, RING, SLAB])
        w_hi = sb("w_hi", [P, RING, SLAB], F32R)
        w_lo = sb("w_lo", [P, RING, SLAB], F32R)
        x = sb("x", [P, NT, D])
        xt_hi = sb("xt_hi", [P, DC, T], F32R)
        xt_lo = sb("xt_lo", [P, DC, T], F32R)
        lng = sb("lng", [P, D])
        lnb = sb("lnb", [P, D])
        stats = sb("stats", [P, 2, 6])
        meanvar = sb("meanvar", [P, NT, 2])
        vareps = sb("vareps", [P, NT])
        rstd = sb("rstd", [P, NT])
        neghalf = sb("neghalf", [P, 8])
        ident = sb("ident", [P, P])
        gate = sb("gate", [P, 2, T])
        hid = sb("hid", [P, 2, T])
        h_hi = sb("h_hi", [P, 2, T], F32R)
        h_lo = sb("h_lo", [P, 2, T], F32R)
        psum = ctx.enter_context(nc.psum_tensor("psum", [P, 8 * T], F32))
        bank = [psum[:, i * T:(i + 1) * T] for i in range(8)]

        arena = sb("arena", [P, ARENA])
        cursor = [0]

        def cut(*shape):
            n = int(np.prod(shape))
            part = arena[:, cursor[0]:cursor[0] + n]
            cursor[0] += n
            assert cursor[0] <= ARENA
            if len(shape) == 2:
                return part.rearrange("p (a b) -> p a b", b=shape[1])
            if len(shape) == 3:
                return part.rearrange("p (a b c) -> p a b c", b=shape[1], c=shape[2])
            return part

        q_t = cut(2, 2, T)
        k_swa = cut(2, T)
        k_moba = cut(2, 2, T)
        v_swa = cut(NT, P)
        v_moba = cut(2, NT, GW)
        dist_swa = cut(7 * P)
        dist_moba = [cut(6 * P), cut(4 * P)]
        probs = cut(2, 7 * P)
        probs_t = cut(2, 7 * P)
        att_out = cut(NT, GW)
        cursor[0] = 0
        decay = cut(2, 2, T)
        qp = cut(2, 2, T)
        ks = cut(2, 2, T)
        values = cut(2, NT, GW)
        out_gate = cut(2, NT, GW)
        block_decay = cut(2 * T)
        squares = block_decay[:, 0:2 * T].rearrange("p (a b) -> p a b", b=P)
        within = cut(2, T)
        keys_tok = cut(2, T)
        normed = keys_tok.rearrange("p h n -> p (h n)").rearrange("p (t n) -> p t n", n=GW)
        state = cut(2, 3, P)
        sig_pos, sig_neg = gate, hid

        neg_max = sb("neg_max", [P, 2, 4])
        sums = sb("sums", [P, 4, 4])
        sink_part = sb("sink_part", [P, 2, 4])
        inv_sum = sb("inv_sum", [P, 4])
        total = sb("total", [P, 4])
        sink_b = sb("sink_b", [P, 8])
        neg_sink = sb("neg_sink", [P, 8])
        norm_b = sb("norm_b", [P, P])
        lb_rows = sb("lb_rows", [16, P])
        lb_t = sb("lb_t", [P, 2, 8])
        lb_m = sb("lb_m", [P, 8])
        lb_e = sb("lb_e", [P, 2, 8])
        lb_r = sb("lb_r", [P, 8])
        lower = sb("lower", [P, 8])
        span = sb("span", [P, 8])
        pair_mask_f = sb("pair_mask_f", [P, 7, 64])
        pair_mask = sb("pair_mask", [P, 7, 64], mybir.dt.uint8)
        mean_sq = sb("mean_sq", [P, 8])
        rms_in = sb("rms_in", [P, 8])
        rms = sb("rms", [P, 8])

        x_loaded = sem("x_loaded")
        ident_zeroed = sem("ident_zeroed")
        consts_ready = sem("consts_ready")
        raw_landed = [sem(f"raw_landed{i}") for i in range(RING)]
        hi_ready = sem("hi_ready")
        lo_ready = sem("lo_ready")
        up1_done = sem("up1_done")
        up3_done = sem("up3_done")
        gate_done = sem("gate_done")
        hid_done = sem("hid_done")
        h_hi_done = sem("h_hi_done")
        h_lo_done = sem("h_lo_done")
        y_done = sem("y_done")
        y_added = sem("y_added")
        par_loaded = [sem(f"par_loaded{i}") for i in range(2)]
        stat_done = sem("stat_done")
        var_ready = sem("var_ready")
        rstd_ready = sem("rstd_ready")
        centred = sem("centred")
        ln_done = sem("ln_done")
        turn_done = sem("turn_done")
        xt_hi_done = sem("xt_hi_done")
        xt_lo_done = sem("xt_lo_done")
        out_stored = sem("out_stored")
        small_loaded = sem("small_loaded")
        lb_turned = sem("lb_turned")
        lb_exp = sem("lb_exp")
        set_up = sem("set_up")
        masks_step = sem("masks_step")
        proj_done = sem("proj_done")
        proj_kept = sem("proj_kept")
        kv_halves = sem("kv_halves")
        kv_copied = [sem(f"kv_copied{i}") for i in range(2)]
        scores_done = sem("scores_done")
        scores_kept = sem("scores_kept")
        max_ready = sem("max_ready")
        neg_max_ready = sem("neg_max_ready")
        exp_done = sem("exp_done")
        probs_turned = sem("probs_turned")
        probs_t_act = sem("probs_t_act")
        probs_t_dve = sem("probs_t_dve")
        head_done = sem("head_done")
        head_kept = sem("head_kept")
        out_turned = sem("out_turned")
        keys_ready = sem("keys_ready")
        level_done = sem("level_done")
        level_kept = sem("level_kept")
        level_step = sem("level_step")
        gate_normed = sem("gate_normed")
        keys_turned = sem("keys_turned")
        keys_tok_ready = sem("keys_tok_ready")
        updates_done = sem("updates_done")
        states_ready = sem("states_ready")
        outputs_done = sem("outputs_done")
        squares_done = sem("squares_done")
        rms_asked = sem("rms_asked")
        rms_ready = sem("rms_ready")
        normed_ready = sem("normed_ready")

        users = []
        for n, ph in enumerate(phases):
            K0 = bases[n][1]
            if ph[0] == "ffn":
                G0 = NG * ffn_index[n]
                users += [(up1_done, 2 * G0 + 2, 2), (up3_done, 2 * G0 + 2, 2)]
                for g in range(1, NG):
                    users += [(up1_done, 2 * (G0 + g) + 2, 2), (y_done, 8 * (K0 + g), 8),
                              (up3_done, 2 * (G0 + g) + 2, 2)]
                users.append((y_done, 8 * (K0 + NG), 8))
            else:
                first_block = BLOCKS * sum(p[0] != "ffn" for p in phases[:n])
                blocks = 0
                for name, g in mixer_schedule(ph[0])[0]:
                    if name == "down":
                        users.append((y_done, 8 * (K0 + g + 1), 8))
                    else:
                        blocks += 2
                        users.append((proj_done, first_block + blocks, 2))

        mixers_before = [sum(p[0] != "ffn" for p in phases[:n]) for n in range(len(phases))]
        block_base = [BLOCKS * m for m in mixers_before]
        out_base = [8 * m for m in mixers_before]

        block = ctx.enter_context(nc.Block())

        def upto(at, i, by=1):
            return at if i is None else at + by * i

        @block.sync
        def _(sp):
            def load_slab(s, src, i=None, view=None):
                if s >= RING or i is not None:
                    sp.wait_ge(lo_ready, upto(s - RING + 1, i, RING))
                dst = raw[:, s % RING, :]
                sp.dma_start(dst.rearrange("p (c n) -> p c n", n=src.shape[-1]), src).then_inc(raw_landed[s % RING], 16)

            def load_params(n):
                l, k = phases[n][2]
                if n:
                    sp.wait_ge(ln_done, NT * n)
                sp.dma_start(lng[:], ln_g[l, k:k + 1, :].broadcast_to([P, D])).then_inc(par_loaded[0], 16)
                sp.dma_start(lnb[:], ln_b[l, k:k + 1, :].broadcast_to([P, D])).then_inc(par_loaded[1], 16)

            def up_slab(w, g):
                return w[:, bass.ds(g * GW, GW)].rearrange("(c p) n -> p c n", p=P)

            def down_slab(w, g):
                return w[bass.ds(g * GW, GW), :].rearrange("(c p) n -> p c n", p=P)

            sp.dma_start(sink_b[:], sinks[0:1, :].broadcast_to([P, 8])).then_inc(small_loaded, 16)
            sp.dma_start(norm_b[:], hnorm[0:1, :].broadcast_to([P, P])).then_inc(small_loaded, 16)
            sp.dma_start(lb_rows[:], lbs_in.rearrange("l (h k) -> (l h) k", k=P)).then_inc(small_loaded, 16)
            if phases[0][0] != "ffn":
                for t in range(NT):
                    sp.dma_start(x[:, t, :], x_in[0, t * P:(t + 1) * P, :]).then_inc(x_loaded, 16)
            for n, (kind, wi, ln, _w) in enumerate(phases):
                s0 = bases[n][0]
                if kind == "ffn":
                    l, f = wi
                    a, b, c = w1[l, f], w3[l, f], w2[l, f]
                    load_slab(s0, up_slab(a, 0))
                    if n == 0:
                        for t in range(NT):
                            sp.dma_start(x[:, t, :], x_in[0, t * P:(t + 1) * P, :]).then_inc(x_loaded, 16)
                    load_slab(s0 + 1, up_slab(b, 0))
                    load_slab(s0 + 2, up_slab(a, 1))
                    load_params(n)
                    load_slab(s0 + 3, down_slab(c, 0))
                    load_slab(s0 + 4, up_slab(b, 1))
                    with sp.Fori(1, NG - 1) as i:
                        load_slab(s0 + 2, up_slab(a, i + 1), i)
                        load_slab(s0 + 3, down_slab(c, i), i)
                        load_slab(s0 + 4, up_slab(b, i + 1), i)
                    load_slab(s0 + 3 * NG - 1, down_slab(c, NG - 1))
                else:
                    for s, (name, g) in enumerate(mixer_schedule(kind)[0]):
                        if s == RING:
                            load_params(n)
                        if kind == "attn":
                            swa, moba = 8 * HD, 8 * HD + 4 * HD
                            col = {"q": g * GW if g < 2 else moba + (g - 2) * GW, "kv": swa,
                                   "kb": moba + 512 + (g - 2) * GW, "vb": moba + 1024 + (g - 2) * GW}
                            src = down_slab(aw_out[0], g) if name == "down" else \
                                aw_in[0][:, col[name]:col[name] + GW].rearrange("(c p) n -> p c n", p=P)
                        else:
                            src = down_slab(hw_out[0], g) if name == "down" else \
                                hw_in[0][:, FQGV[name] * D + g * GW:FQGV[name] * D + (g + 1) * GW]\
                                .rearrange("(c p) n -> p c n", p=P)
                        load_slab(s0 + s, src)
            for t in range(NT):
                sp.wait_ge(ln_done, NT * last_phase + t + 1)
                sp.dma_start(out[0, t * P:(t + 1) * P, :], x[:, t, :]).then_inc(out_stored, 16)
            sp.wait_ge(out_stored, 16 * NT)

        @block.gpsimd
        def _(pool):
            pool.memset(neghalf[:], -0.5).then_inc(consts_ready, 1)
            pool.memset(ident[:], 0.0).then_inc(ident_zeroed, 1)
            pool.wait_ge(ident_zeroed, 1)
            pool.affine_select(out=ident[:], in_=ident[:], compare_op=ALU.not_equal, fill=1.0, base=0,
                               pattern=[[-1, P]], channel_multiplier=1).then_inc(consts_ready, 1)

            steps = [0]

            def then(op):
                op.then_inc(masks_step, 1)
                steps[0] += 1
                pool.wait_ge(masks_step, steps[0])

            def distances(table, tile, keys, window):
                n = len(keys) * P
                then(pool.iota(table, pattern=[[-1, n]], base=(tile - keys[0]) * P, channel_multiplier=1,
                               allow_small_or_imprecise_dtypes=True))
                then(pool.affine_select(out=table, in_=table, compare_op=ALU.is_ge, fill=FAR,
                                        base=(tile - keys[0]) * P, pattern=[[-1, n]], channel_multiplier=1))
                if window:
                    then(pool.affine_select(out=table, in_=table, compare_op=ALU.is_ge, fill=FAR,
                                            base=WINDOW - 1 - (tile - keys[0]) * P, pattern=[[1, n]],
                                            channel_multiplier=-1))

            def attention_tables():
                for table, (tiles, _) in [(dist_swa, SWA_UNIT), (dist_moba[0], MOBA_UNITS[0]), (dist_moba[1], MOBA_UNITS[1])]:
                    at = 0
                    for tile, keys in tiles:
                        distances(table[:, at:at + len(keys) * P], tile, keys, table is dist_swa)
                        at += len(keys) * P

            then(pool.memset(pair_mask_f[:], 1.0))
            for a, m in enumerate(LEVELS):
                view = pair_mask_f[:, a, :].rearrange("p (b e) -> p b e", e=m)
                then(pool.affine_select(out=view, in_=view, compare_op=ALU.is_ge, fill=0.0, base=0,
                                        pattern=[[-2 * m, 64 // m], [0, m]], channel_multiplier=1))
                then(pool.affine_select(out=view, in_=view, compare_op=ALU.is_ge, fill=0.0, base=m - 1,
                                        pattern=[[2 * m, 64 // m], [0, m]], channel_multiplier=-1))

            def low(s, i=None):
                pool.wait_ge(hi_ready, upto(s + 1, i, RING))
                pool.tensor_tensor(w_lo[:, s % RING, :], raw[:, s % RING, :], w_hi[:, s % RING, :].bitcast(F32),
                                   ALU.subtract).then_inc(lo_ready, 1)

            def norm_powers(n):
                for t in range(NT):
                    pool.wait_ge(var_ready, NT * n + t + 1)
                    pool.tensor_tensor(rstd[:, t:t + 1], vareps[:, t:t + 1], neghalf[:, 0:1],
                                       ALU.pow).then_inc(rstd_ready, 1)

            for s in range(min(RING, n_slabs)):
                low(s)
            for n, (kind, wi, ln, _w) in enumerate(phases):
                s0 = bases[n][0]
                if kind == "ffn":
                    with pool.Fori(0, NG - 1) as i:
                        for j in range(RING):
                            low(s0 + RING + j, i)
                    if n < last_phase:
                        for s in range(s0 + 3 * NG, s0 + 3 * NG + 2):
                            low(s)
                    norm_powers(n)
                    if n < last_phase:
                        low(s0 + 3 * NG + 2)
                else:
                    slabs, plan = mixer_schedule(kind)
                    if kind == "attn":
                        attention_tables()
                    for step in plan:
                        if step[0] == "quarter" and step[2] == 3 and s0 + step[1] + RING < n_slabs:
                            low(s0 + step[1] + RING)
                        if step[0] == "quarter" and step[2] == 3 and slabs[step[1]][0] == "g":
                            g = slabs[step[1]][1]
                            pool.wait_ge(small_loaded, 48)
                            pool.wait_ge(proj_kept, block_base[n] + 8 * g + 6)
                            view = out_gate[:, g % 2].rearrange("p t (h n) -> p (t h) n", n=P)
                            pool.tensor_tensor(view, view, norm_b[:, None, :].broadcast_to([P, 8, P]),
                                               ALU.mult).then_inc(gate_normed, 1)
                        if step[0] == "outputs":
                            pool.wait_ge(rms_asked, step[1] + 1)
                            pool.tensor_tensor(rms[:], rms_in[:], neghalf[:], ALU.pow).then_inc(rms_ready, 1)
                    norm_powers(n)
                    if s0 + len(slabs) + 2 < n_slabs:
                        low(s0 + len(slabs) + 2)

        @block.scalar
        def _(act):
            def high(s, i=None):
                act.wait_ge(raw_landed[s % RING], upto(16 * (s // RING + 1), i, 16))
                if s >= RING:
                    used, count, by = users[s - RING]
                    act.wait_ge(used, upto(count, i, by))
                act.activation(w_hi[:, s % RING, :], raw[:, s % RING, :], ACT.Copy).then_inc(hi_ready, 1)

            def turn_high(turn, t):
                for b in range(2):
                    act.wait_ge(turn_done, 8 * turn + 2 * t + b + 1)
                    act.activation(xt_hi[:, 4 * b:4 * b + 4, t * P:(t + 1) * P],
                                   bank[2 * (t % 2) + b][:].rearrange("p (c n) -> p c n", n=P),
                                   ACT.Copy).then_inc(xt_hi_done, 1)

            def gates(G, i=None):
                for j in range(2):
                    act.wait_ge(up1_done, upto(2 * G + j + 1, i, 2))
                    if G:
                        act.wait_ge(hid_done, upto(2 * (G - 1) + j + 1, i, 2))
                    act.activation(gate[:, j, :], bank[j][:], ACT.Silu).then_inc(gate_done, 1)

            def hid_high(G, K, i=None):
                for j in range(2):
                    act.wait_ge(hid_done, upto(2 * G + j + 1, i, 2))
                    if K:
                        act.wait_ge(y_done, upto(8 * K, i, 8))
                    act.activation(h_hi[:, j, :], hid[:, j, :], ACT.Copy).then_inc(h_hi_done, 1)

            high(0)
            high(1)
            act.wait_ge(lb_turned, 1)
            act.activation(lb_t[:].rearrange("p l h -> p (l h)"), bank[7][:, 0:16], ACT.Copy).then_inc(lb_exp, 1)
            act.wait_ge(set_up, 2)
            act.activation(lb_e[:], lb_t[:], ACT.Exp).then_inc(lb_exp, 1)
            for t in range(NT):
                turn_high(0, t)
            high(2)

            def keep_block(kind, slabs, s, j, block):
                name, g = slabs[s]
                src = bank[block % 2]
                two_tiles = src.rearrange("p (t n) -> p t n", n=GW)
                act.wait_ge(proj_done, block + 1)
                if name == "q" and kind == "attn":
                    op = act.activation(q_t[:, g % 2, j, :], src, ACT.Copy, scale=SCALE)
                elif name == "kv" and j == 0:
                    act.activation(k_swa[0:HD, 0, :], src[0:HD, :], ACT.Copy).then_inc(kv_halves, 1)
                    op = act.activation(k_swa[HD:P, 1, :], src[HD:P, :], ACT.Copy)
                elif name == "kv":
                    op = act.activation(v_swa, src.rearrange("p (t n) -> p t n", n=P), ACT.Copy)
                elif name == "kb":
                    op = act.activation(k_moba[:, g % 2, j, :], src, ACT.Copy)
                elif name == "vb":
                    op = act.activation(v_moba[:, g % 2, 2 * j:2 * j + 2, :], two_tiles, ACT.Copy)
                elif name == "f":
                    if g:
                        act.wait_ge(keys_ready, 2 * (g - 1) + j + 1)
                    act.activation(sig_pos[:, j, :], src, ACT.Sigmoid)
                    op = act.activation(sig_neg[:, j, :], src, ACT.Sigmoid, scale=-1.0)
                elif name == "q":
                    op = act.activation(qp[:, g % 2, j, :], src, ACT.Silu)
                elif name == "g":
                    op = act.activation(out_gate[:, g % 2, 2 * j:2 * j + 2, :], two_tiles, ACT.Silu)
                else:
                    op = act.activation(values[:, g % 2, 2 * j:2 * j + 2, :], two_tiles, ACT.Copy)
                op.then_inc(proj_kept, 1)
                if name == "kv" and j == 0:
                    act.wait_ge(kv_halves, 1)
                    act.dma_start(k_swa[HD:P, 0, :], k_swa[0:HD, 0, :]).then_inc(kv_copied[0], 16)
                    act.wait_ge(proj_kept, block + 1)
                    act.dma_start(k_swa[0:HD, 1, :], k_swa[HD:P, 1, :]).then_inc(kv_copied[1], 16)

            def exponentials(u):
                head, tiles, _, _ = attention_unit(u)
                act.wait_ge(neg_max_ready, u + 1)
                at = 0
                for n_, (tile, keys) in enumerate(tiles):
                    part = probs[:, u % 2, at:at + len(keys) * P]
                    op = act.activation(part, part, ACT.Exp, bias=neg_max[:, u % 2, n_:n_ + 1],
                                        accum_out=sums[:, head % 4, tile:tile + 1])
                    at += len(keys) * P
                if head < 8:
                    op = act.activation(sink_part[:, head % 2, :], neg_max[:, u % 2, :], ACT.Exp,
                                        bias=sink_b[:, head:head + 1])
                op.then_inc(exp_done, 1)

            def probs_first_bank(u):
                act.wait_ge(probs_turned, u + 1)
                act.activation(probs_t[:, u % 2, 0:4 * P], bank[4], ACT.Copy).then_inc(probs_t_act, 1)

            def turned_out_high(first_bank, outs, K):
                for j in range(2):
                    act.wait_ge(out_turned, outs + j + 1)
                    if K:
                        act.wait_ge(y_done, 8 * K)
                    act.activation(h_hi[:, j, :], bank[first_bank + j], ACT.Copy).then_inc(h_hi_done, 1)
            for n, (kind, wi, ln, _w) in enumerate(phases):
                s0, K0 = bases[n]
                if kind == "ffn":
                    G0 = NG * ffn_index[n]
                    gates(G0)
                    high(s0 + 3)
                    hid_high(G0, K0)
                    high(s0 + 4)
                    with act.Fori(0, NG - 2) as i:
                        gates(G0 + 1, i)
                        high(s0 + 5, i)
                        high(s0 + 6, i)
                        hid_high(G0 + 1, K0 + 1, i)
                        high(s0 + 7, i)
                    gates(G0 + NG - 1)
                    high(s0 + 3 * NG - 1)
                    if n < last_phase:
                        high(s0 + 3 * NG)
                    hid_high(G0 + NG - 1, K0 + NG - 1)
                    if n < last_phase:
                        high(s0 + 3 * NG + 1)
                else:
                    slabs, plan = mixer_schedule(kind)
                    block, outs = block_base[n], out_base[n]
                    for step in plan:
                        if step[0] == "quarter":
                            name = slabs[step[1]][0]
                            if name != "down" and step[2] % 2 == 1:
                                keep_block(kind, slabs, step[1], step[2] // 2, block)
                                block += 1
                            if step[2] == 3 and s0 + step[1] + RING < n_slabs:
                                high(s0 + step[1] + RING)
                        elif step[0] == "scores":
                            exponentials(step[1])
                        elif step[0] == "turn_probs":
                            probs_first_bank(step[1])
                        elif step[0] == "turn_keys":
                            for h in range(2):
                                act.wait_ge(keys_turned, 2 * step[1] + h + 1)
                                act.activation(keys_tok[:, h, :], bank[4 + h], ACT.Copy).then_inc(keys_tok_ready, 1)
                        elif step[0] == "outputs":
                            for b in range(2):
                                act.wait_ge(outputs_done, 2 * step[1] + b + 1)
                                act.activation(squares[:, 4 * b:4 * b + 4, :],
                                               bank[4 + b].rearrange("p (a n) -> p a n", n=P),
                                               ACT.Square).then_inc(squares_done, 1)
                        elif step[0] == "turn_out":
                            turned_out_high(4 if kind == "attn" else 2, outs + 2 * step[1], K0 + step[1])
                if n < last_phase:
                    turn_high(n + 1, 0)
                    turn_high(n + 1, 1)
                    high(bases[n + 1][0] + 2)
                    turn_high(n + 1, 2)
                    turn_high(n + 1, 3)

        @block.vector
        def _(dve):
            def turn_low(turn, t):
                for b in range(2):
                    dve.wait_ge(xt_hi_done, 8 * turn + 2 * t + b + 1)
                    part = (slice(None), slice(4 * b, 4 * b + 4), slice(t * P, (t + 1) * P))
                    dve.tensor_tensor(xt_lo[part], bank[2 * (t % 2) + b][:].rearrange("p (c n) -> p c n", n=P),
                                      xt_hi[part].bitcast(F32), ALU.subtract).then_inc(xt_lo_done, 1)

            def hiddens(G, i=None):
                for j in range(2):
                    dve.wait_ge(gate_done, upto(2 * G + j + 1, i, 2))
                    dve.wait_ge(up3_done, upto(2 * G + j + 1, i, 2))
                    dve.tensor_tensor(hid[:, j, :], bank[2 + j][:], gate[:, j, :], ALU.mult).then_inc(hid_done, 1)

            def hid_low(K, i=None):
                for j in range(2):
                    dve.wait_ge(h_hi_done, upto(2 * K + j + 1, i, 2))
                    dve.tensor_tensor(h_lo[:, j, :], hid[:, j, :], h_hi[:, j, :].bitcast(F32),
                                      ALU.subtract).then_inc(h_lo_done, 1)

            def add_piece(K, k, weight, banks, i=None):
                t, half = divmod(k, 2)
                dve.wait_ge(y_done, upto(8 * K + k + 1, i, 8))
                part = x[:, t, half * HALF:(half + 1) * HALF]
                dve.scalar_tensor_tensor(out=part, in0=banks[k % len(banks)][:], scalar=weight / ALPHA, in1=part,
                                         op0=ALU.mult, op1=ALU.add).then_inc(y_added, 1)

            chain = [0]

            def then(op):
                op.then_inc(stat_done, 1)
                chain[0] += 1
                dve.wait_ge(stat_done, chain[0])

            def logits(u):
                head, tiles, col, _ = attention_unit(u)
                width = sum(len(keys) for _, keys in tiles) * P
                table = dist_swa if u < 8 else dist_moba[u % 2]
                dve.wait_ge(scores_done, u + 1)
                if u >= 2:
                    dve.wait_ge(probs_turned, u - 1)
                lg = probs[:, u % 2, 0:width]
                dve.scalar_tensor_tensor(out=lg, in0=table, scalar=-SLOPES[head],
                                         in1=psum[:, 2 * T + col:2 * T + col + width],
                                         op0=ALU.mult, op1=ALU.add).then_inc(scores_kept, 1)
                dve.wait_ge(scores_kept, u + 1)
                at = 0
                for n_, (tile, keys) in enumerate(tiles):
                    op = dve.tensor_reduce(neg_max[:, u % 2, n_:n_ + 1], probs[:, u % 2, at:at + len(keys) * P],
                                           AX.X, ALU.max, negate=True)
                    at += len(keys) * P
                if head < 8:
                    op.then_inc(max_ready, 1)
                    dve.wait_ge(max_ready, u + 1)
                    op = dve.tensor_scalar(neg_max[:, u % 2, :], neg_max[:, u % 2, :], neg_sink[:, head:head + 1],
                                           None, ALU.min)
                op.then_inc(neg_max_ready, 1)

            def probs_second_bank(u):
                blocks = sum(len(keys) for _, keys in attention_unit(u)[1])
                if blocks > 4:
                    dve.wait_ge(probs_turned, u + 1)
                    dve.tensor_copy(probs_t[:, u % 2, 4 * P:blocks * P],
                                    bank[5][:, 0:(blocks - 4) * P]).then_inc(probs_t_dve, 1)

            def keep_head(u):
                head, _, _, ends = attention_unit(u)
                if not ends:
                    return
                dve.wait_ge(head_done, head + 1)
                dve.wait_ge(exp_done, u + 1)
                sum_ = sums[:, head % 4, :]
                if head < 8:
                    then(dve.tensor_tensor(total[:], sum_, sink_part[:, head % 2, :], ALU.add))
                    sum_ = total[:]
                then(dve.reciprocal(inv_sum[:], sum_))
                dve.tensor_tensor(att_out[:, :, (head % 4) * HD:(head % 4 + 1) * HD],
                                  bank[6 + head % 2][:, 0:NT * HD].rearrange("p (t n) -> p t n", n=HD),
                                  inv_sum[:, :, None].broadcast_to([P, NT, HD]), ALU.mult).then_inc(head_kept, 1)

            def decays_and_keys(g, j, first_block):
                head = 2 * g + j
                dve.wait_ge(proj_kept, first_block + 8 * g + j + 1)
                dve.tensor_scalar(decay[:, g % 2, j, :], sig_pos[:, j, :], span[:, head:head + 1],
                                  lower[:, head:head + 1], ALU.mult, ALU.add)
                dve.tensor_scalar(ks[:, g % 2, j, :], sig_neg[:, j, :], span[:, head:head + 1], None,
                                  ALU.mult).then_inc(keys_ready, 1)

            def level(g, a):
                q_, k_, par = qp[:, g % 2], ks[:, g % 2], g % 2
                dve.wait_ge(level_done, 8 * g + a + 1)
                if a == 0:
                    for h in range(2):
                        dve.tensor_tensor(within[:, h, :].rearrange("p (c t) -> p c t", t=P),
                                          bank[2 + h].rearrange("p (c t) -> p c t", t=P),
                                          ident[:, None, :].broadcast_to([P, 4, P]), ALU.mult)
                    dve.tensor_tensor(q_, q_, decay[:, par], ALU.mult).then_inc(level_kept, 1)
                    dve.wait_ge(level_kept, 8 * g + 1)
                    return
                m = LEVELS[a - 1]
                n_ = T // (2 * m)
                pairs = "p h (b two e) -> p (h b) two e"
                at = within[:].rearrange(pairs, two=2, e=m)[:, :, 1, :]
                dst = at.rearrange("p (x b) e -> p x b e", b=64 // m)
                dve.copy_predicated(dst, pair_mask[:, a - 1, :].rearrange("p (b e) -> p b e", e=m)[:, None, :, :]
                                    .broadcast_to([P, 8, 64 // m, m]),
                                    bank[2 + a % 2].rearrange("p (x b e) -> p x b e", b=64 // m, e=m))
                old = decay[:, par].rearrange("p h t -> p (h t)") if m == 1 else \
                    block_decay[:, decay_at(m):decay_at(m) + 2 * T // m]
                old = old.rearrange("p (b two) -> p b two", two=2)
                qv = q_.rearrange(pairs, two=2, e=m)[:, :, 1, :]
                kv = k_.rearrange(pairs, two=2, e=m)[:, :, 0, :]
                dve.tensor_tensor(qv, qv, old[:, :, 0:1].broadcast_to([P, 2 * n_, m]), ALU.mult)
                dve.tensor_tensor(kv, kv, old[:, :, 1:2].broadcast_to([P, 2 * n_, m]), ALU.mult)
                dve.tensor_tensor(block_decay[:, decay_at(2 * m):decay_at(2 * m) + 2 * n_], old[:, :, 0],
                                  old[:, :, 1], ALU.mult).then_inc(level_kept, 1)
                dve.wait_ge(level_kept, 8 * g + a + 1)

            def states(g):
                dve.wait_ge(updates_done, g + 1)
                for c in range(3):
                    for h in range(2):
                        upd = bank[2 + h][:, c * P:(c + 1) * P]
                        if c == 0:
                            op = dve.tensor_copy(state[:, h, 0, :], upd)
                        else:
                            whole = block_decay[:, decay_at(P) + 4 * h + c:decay_at(P) + 4 * h + c + 1]
                            op = dve.scalar_tensor_tensor(out=state[:, h, c, :], in0=state[:, h, c - 1, :],
                                                          scalar=whole, in1=upd, op0=ALU.mult, op1=ALU.add)
                    if c < 2:
                        then(op)
                op.then_inc(states_ready, 1)

            def norm_outputs(g):
                dve.wait_ge(squares_done, 2 * g + 2)
                then(dve.tensor_reduce(mean_sq[:], squares, AX.X, ALU.add))
                dve.tensor_scalar(rms_in[:], mean_sq[:], 1.0 / P, RMS_EPS, ALU.mult, ALU.add).then_inc(rms_asked, 1)
                dve.wait_ge(rms_ready, g + 1)
                dve.wait_ge(gate_normed, g + 1)
                dve.wait_ge(keys_tok_ready, 2 * g + 2)
                for t in range(NT):
                    for h in range(2):
                        op = dve.scalar_tensor_tensor(
                            out=normed[:, t, h * P:(h + 1) * P],
                            in0=bank[4 + t // 2][:, (t % 2) * GW + h * P:(t % 2) * GW + (h + 1) * P],
                            scalar=rms[:, 2 * t + h:2 * t + h + 1], in1=out_gate[:, g % 2, t, h * P:(h + 1) * P],
                            op0=ALU.mult, op1=ALU.mult)
                op.then_inc(normed_ready, 1)

            def last_down_and_norm(n, K, weight, banks):
                for t in range(NT):
                    add_piece(K, 2 * t, weight, banks)
                    add_piece(K, 2 * t + 1, weight, banks)
                    dve.wait_ge(y_added, FREE_AT_START + 8 * K + 2 * t + 1)
                    dve.bn_stats(stats[:, 0, :], x[:, t, 0:HALF])
                    dve.wait_ge(y_added, FREE_AT_START + 8 * K + 2 * t + 2)
                    then(dve.bn_stats(stats[:, 1, :], x[:, t, HALF:D]))
                    then(dve.bn_aggr(meanvar[:, t, :], stats[:, :, :]))
                    dve.tensor_scalar(vareps[:, t:t + 1], meanvar[:, t, 1:2], LN_EPS, None,
                                      ALU.add).then_inc(var_ready, 1)
                    if t == 0:
                        dve.wait_ge(par_loaded[0], 16 * (n + 1))
                        dve.wait_ge(par_loaded[1], 16 * (n + 1))
                    dve.scalar_tensor_tensor(out=x[:, t, :], in0=x[:, t, :], scalar=meanvar[:, t, 0:1],
                                             in1=lng[:], op0=ALU.subtract,
                                             op1=ALU.mult).then_inc(centred, 1)
                    if t and n < last_phase:
                        turn_low(n + 1, t - 1)
                    dve.wait_ge(centred, NT * n + t + 1)
                    dve.wait_ge(rstd_ready, NT * n + t + 1)
                    dve.scalar_tensor_tensor(out=x[:, t, :], in0=x[:, t, :], scalar=rstd[:, t:t + 1],
                                             in1=lnb[:], op0=ALU.mult, op1=ALU.add).then_inc(ln_done, 1)
                if n < last_phase:
                    turn_low(n + 1, NT - 1)

            dve.memset(stats[:], 0.0).then_inc(y_added, FREE_AT_START)
            dve.wait_ge(lb_exp, 1)
            dve.tensor_tensor(lb_m[:], lb_t[:, 0, :], lb_t[:, 1, :], ALU.max).then_inc(set_up, 1)
            dve.wait_ge(set_up, 1)
            dve.tensor_tensor(lb_t[:], lb_t[:], lb_m[:, None, :].broadcast_to([P, 2, 8]),
                              ALU.subtract).then_inc(set_up, 1)
            dve.wait_ge(lb_exp, 2)
            dve.tensor_tensor(lb_m[:], lb_e[:, 0, :], lb_e[:, 1, :], ALU.add).then_inc(set_up, 1)
            dve.wait_ge(set_up, 3)
            dve.reciprocal(lb_r[:], lb_m[:]).then_inc(set_up, 1)
            dve.wait_ge(set_up, 4)
            dve.tensor_tensor(lower[:], lb_e[:, 1, :], lb_r[:], ALU.mult)
            dve.tensor_tensor(span[:], lb_e[:, 0, :], lb_r[:], ALU.mult)
            dve.wait_ge(small_loaded, 48)
            dve.tensor_scalar(neg_sink[:], sink_b[:], -1.0, None, ALU.mult)
            dve.wait_ge(masks_step, MASK_STEPS)
            dve.tensor_copy(pair_mask[:], pair_mask_f[:]).then_inc(set_up, 1)
            dve.wait_ge(set_up, 5)
            for t in range(NT):
                turn_low(0, t)
            for n, (kind, wi, ln, weight) in enumerate(phases):
                s0, K0 = bases[n]
                if kind == "ffn":
                    G0 = NG * ffn_index[n]
                    hiddens(G0)
                    hid_low(K0)
                    with dve.Fori(0, NG - 1) as i:
                        for k in range(8):
                            add_piece(K0, k, weight, bank[4:8], i)
                        hiddens(G0 + 1, i)
                        hid_low(K0 + 1, i)
                    last_down_and_norm(n, K0 + NG - 1, weight, bank[4:8])
                else:
                    slabs, plan = mixer_schedule(kind)
                    banks = bank[0:2] if kind == "attn" else bank[6:8]
                    outs = out_base[n]
                    if kind == "attn":
                        dve.wait_ge(masks_step, MASK_STEPS + TABLE_STEPS)
                    for step in plan:
                        if step[0] == "quarter":
                            name, g = slabs[step[1]]
                            if name == "down":
                                add_piece(K0 + g, 2 * step[2], weight, banks)
                                add_piece(K0 + g, 2 * step[2] + 1, weight, banks)
                            if name == "f" and step[2] % 2 == 1:
                                decays_and_keys(g, step[2] // 2, block_base[n])
                        elif step[0] == "scores":
                            logits(step[1])
                        elif step[0] == "turn_probs":
                            probs_second_bank(step[1])
                        elif step[0] == "values":
                            keep_head(step[1])
                        elif step[0] == "level":
                            level(step[1], step[2])
                        elif step[0] == "updates":
                            states(step[1])
                        elif step[0] == "outputs":
                            norm_outputs(step[1])
                        elif step[0] == "turn_out":
                            for j in range(2):
                                dve.wait_ge(h_hi_done, 2 * (K0 + step[1]) + j + 1)
                                dve.tensor_tensor(h_lo[:, j, :], bank[(4 if kind == "attn" else 2) + j],
                                                  h_hi[:, j, :].bitcast(F32), ALU.subtract).then_inc(h_lo_done, 1)
                    last_down_and_norm(n, K0 + 3, weight, bank[4:8])

        @block.tensor
        def _(pe):
            def three(out_, w, xs, first, last):
                pe.matmul(out_, w[0], xs[0], start=first, stop=False)
                pe.matmul(out_, w[0], xs[1], start=False, stop=False)
                return pe.matmul(out_, w[1], xs[0], start=False, stop=last)

            def features(out_, slot, j, tok):
                for c in range(DC):
                    cols = slice(c * GW + j * P, c * GW + (j + 1) * P)
                    mm = three(out_, (w_hi[:, slot, cols], w_lo[:, slot, cols]),
                               (xt_hi[:, c, tok], xt_lo[:, c, tok]), c == 0, c == DC - 1)
                return mm

            def turn(turn_no, t):
                if t >= 2:
                    pe.wait_ge(xt_lo_done, 8 * turn_no + 2 * (t - 1))
                for b in range(2):
                    for c in range(4):
                        mm = pe.transpose(bank[2 * (t % 2) + b][:, c * P:(c + 1) * P],
                                          x[:, t, (4 * b + c) * P:(4 * b + c + 1) * P], ident[:])
                    mm.then_inc(turn_done, 1)

            def up(s, G, done, freed, b0, i=None, parts=1, turn_no=None):
                pe.wait_ge(lo_ready, upto(s + 1, i, RING))
                if G:
                    pe.wait_ge(freed, upto(2 * G, i, 2))
                n = T // parts
                for h in range(parts):
                    if turn_no is not None:
                        pe.wait_ge(xt_lo_done, 8 * turn_no + (8 // parts) * (h + 1))
                    for j in range(2):
                        tok = slice(h * n, (h + 1) * n)
                        mm = features(bank[b0 + j][:, tok], s % RING, j, tok)
                        if h == parts - 1 and j == 0:
                            mm.then_inc(done, 1)
                mm.then_inc(done, 1)
                return mm

            def down(s, K, banks, i=None):
                for t in range(NT):
                    down_quarter(s, K, t, banks, i)

            def down_quarter(s, K, t, banks, i=None):
                slot = s % RING
                if t == 0:
                    pe.wait_ge(lo_ready, upto(s + 1, i, RING))
                    pe.wait_ge(h_lo_done, upto(2 * K + 2, i, 2))
                for k in (2 * t, 2 * t + 1):
                    half = k % 2
                    pe.wait_ge(y_added, upto(8 * K + k + 1 + FREE_AT_START - len(banks), i, 8))
                    tok = slice(t * P, (t + 1) * P)
                    for c in range(2):
                        cols = slice(c * D + half * HALF, c * D + (half + 1) * HALF)
                        mm = three(banks[k % len(banks)][:], (h_hi[:, c, tok], h_lo[:, c, tok]),
                                   (w_hi[:, slot, cols], w_lo[:, slot, cols]), c == 0, c == 1)
                    mm.then_inc(y_done, 1)

            def projected(s, name, kind, quarter, block, g):
                slot = s % RING
                j, half = divmod(quarter, 2)
                if quarter == 0:
                    pe.wait_ge(lo_ready, s + 1)
                if half == 0 and block >= 2:
                    pe.wait_ge(proj_kept, block - 1)
                out_ = bank[block % 2]
                token_major = name in ("v", "g", "vb") or (name == "kv" and j == 1)
                if not token_major:
                    for c in range(4 * half, 4 * half + 4):
                        cols = slice(c * GW + j * P, c * GW + (j + 1) * P)
                        mm = three(out_, (w_hi[:, slot, cols], w_lo[:, slot, cols]),
                                   (xt_hi[:, c, :], xt_lo[:, c, :]), c == 0, c == DC - 1)
                else:
                    n_, first_col = (P, P) if name == "kv" else (GW, 0)
                    tiles = [2 * half, 2 * half + 1] if name == "kv" else [2 * j + half]
                    for t in tiles:
                        at = (t if name == "kv" else t % 2) * n_
                        tok = slice(t * P, (t + 1) * P)
                        for c in range(DC):
                            cols = slice(c * GW + first_col, c * GW + first_col + n_)
                            mm = three(out_[:, at:at + n_], (xt_hi[:, c, tok], xt_lo[:, c, tok]),
                                       (w_hi[:, slot, cols], w_lo[:, slot, cols]), c == 0, c == DC - 1)
                if half == 1:
                    mm.then_inc(proj_done, 1)

            def scores(u, blocks_needed):
                head, tiles, col, _ = attention_unit(u)
                g = head // 4
                rows = slice((head % 2) * HD, (head % 2 + 1) * HD)
                if u:
                    pe.wait_ge(scores_kept, u)
                pe.wait_ge(proj_kept, blocks_needed)
                if u == 0:
                    pe.wait_ge(kv_copied[0], 16)
                    pe.wait_ge(kv_copied[1], 16)
                at = 2 * T + col
                for tile, keys in tiles:
                    kt = k_swa[rows, g, :] if head < 8 else k_moba[rows, g % 2, (head % 4) // 2, :]
                    mm = pe.matmul(psum[:, at:at + len(keys) * P],
                                   q_t[rows, g % 2, (head % 4) // 2, tile * P:(tile + 1) * P],
                                   kt[:, keys[0] * P:(keys[-1] + 1) * P], start=True, stop=True)
                    at += len(keys) * P
                mm.then_inc(scores_done, 1)

            def turn_probs(u, K):
                blocks = sum(len(keys) for _, keys in attention_unit(u)[1])
                pe.wait_ge(exp_done, u + 1)
                if u:
                    pe.wait_ge(probs_t_act, u)
                    pe.wait_ge(probs_t_dve, two_bank_units(u))
                pe.wait_ge(h_lo_done, 2 * K) if K else None
                for b in range(blocks):
                    mm = pe.transpose(psum[:, 4 * T + b * P:4 * T + (b + 1) * P],
                                      probs[:, u % 2, b * P:(b + 1) * P], ident[:])
                mm.then_inc(probs_turned, 1)

            def weigh_values(u):
                head, tiles, _, ends = attention_unit(u)
                pe.wait_ge(probs_t_act, u + 1)
                pe.wait_ge(probs_t_dve, two_bank_units(u + 1))
                if head >= 2:
                    pe.wait_ge(head_kept, head - 1)
                b = 0
                for tile, keys in tiles:
                    for key in keys:
                        v_ = v_swa[:, key, (head // 4) * HD:(head // 4 + 1) * HD] if head < 8 else \
                            v_moba[:, (head // 4) % 2, key, (head % 4) * HD:(head % 4 + 1) * HD]
                        mm = pe.matmul(bank[6 + head % 2][:, tile * HD:(tile + 1) * HD],
                                       probs_t[:, u % 2, b * P:(b + 1) * P], v_,
                                       start=key == keys[0], stop=key == keys[-1])
                        b += 1
                if ends:
                    mm.then_inc(head_done, 1)

            def level_products(g, a, blocks_needed):
                if a == 0:
                    pe.wait_ge(proj_kept, blocks_needed)
                    pe.wait_ge(keys_ready, 2 * g + 2)
                    if g:
                        pe.wait_ge(h_lo_done, 2 * h_base + 2 * g)
                else:
                    pe.wait_ge(level_kept, 8 * g + a)
                for h in range(2):
                    for c in range(4):
                        chunk = slice(c * P, (c + 1) * P)
                        if a == 0:
                            out_, rhs = bank[2 + h][:, chunk], qp[:, g % 2, h, chunk]
                        else:
                            m = LEVELS[a - 1]
                            out_ = bank[2 + a % 2][:, (4 * h + c) * 64:(4 * h + c + 1) * 64]
                            rhs = qp[:, g % 2, h, chunk].rearrange("p (b two e) -> p b two e", two=2, e=m)[:, :, 1, :]
                        mm = pe.matmul(out_, ks[:, g % 2, h, chunk], rhs, start=True, stop=True)
                mm.then_inc(level_done, 1)

            def turn_keys(g):
                pe.wait_ge(level_kept, 8 * g + 8)
                if g:
                    pe.wait_ge(normed_ready, g)
                for h in range(2):
                    for c in range(4):
                        mm = pe.transpose(bank[4 + h][:, c * P:(c + 1) * P], ks[:, g % 2, h, c * P:(c + 1) * P], ident[:])
                    mm.then_inc(keys_turned, 1)

            def updates(g, blocks_needed):
                pe.wait_ge(keys_tok_ready, 2 * g + 2)
                pe.wait_ge(proj_kept, blocks_needed)
                for h in range(2):
                    for c in range(3):
                        mm = pe.matmul(bank[2 + h][:, c * P:(c + 1) * P], keys_tok[:, h, c * P:(c + 1) * P],
                                       values[:, g % 2, c, h * P:(h + 1) * P], start=True, stop=True)
                mm.then_inc(updates_done, 1)

            def outputs(g):
                pe.wait_ge(states_ready, g + 1)
                for c in range(4):
                    for h in range(2):
                        out_ = bank[4 + c // 2][:, (c % 2) * GW + h * P:(c % 2) * GW + (h + 1) * P]
                        chunk = slice(c * P, (c + 1) * P)
                        mm = pe.matmul(out_, within[:, h, chunk], values[:, g % 2, c, h * P:(h + 1) * P],
                                       start=True, stop=c == 0)
                        if c:
                            mm = pe.matmul(out_, qp[:, g % 2, h, chunk], state[:, h, c - 1, :], start=False, stop=True)
                    if c % 2:
                        mm.then_inc(outputs_done, 1)

            def turn_out(src, first_bank):
                for j in range(2):
                    for t in range(NT):
                        mm = pe.transpose(bank[first_bank + j][:, t * P:(t + 1) * P], src[:, t, j * P:(j + 1) * P], ident[:])
                    mm.then_inc(out_turned, 1)

            pe.wait_ge(consts_ready, 2)
            pe.wait_ge(small_loaded, 48)
            pe.transpose(bank[7][:, 0:16], lb_rows[:], ident[0:16, 0:16]).then_inc(lb_turned, 1)
            for t in range(NT):
                pe.wait_ge(x_loaded, 16 * NT)
                turn(0, t)
            for n, (kind, wi, ln, _w) in enumerate(phases):
                s0, K0 = bases[n]
                if kind == "ffn":
                    G0 = NG * ffn_index[n]
                    up(s0, G0, up1_done, gate_done, 0, turn_no=n)
                    up(s0 + 1, G0, up3_done, hid_done, 2)
                    with pe.Fori(0, NG - 1) as i:
                        up(s0 + 2, G0 + 1, up1_done, gate_done, 0, i)
                        down(s0 + 3, K0, bank[4:8], i)
                        up(s0 + 4, G0 + 1, up3_done, hid_done, 2, i)
                    down(s0 + 3 * NG - 1, K0 + NG - 1, bank[4:8])
                else:
                    slabs, plan = mixer_schedule(kind)
                    banks = bank[0:2] if kind == "attn" else bank[6:8]
                    first, block = block_base[n], block_base[n]
                    h_base = K0
                    pe.wait_ge(xt_lo_done, 8 * (n + 1))
                    for step in plan:
                        if step[0] == "quarter":
                            name, g = slabs[step[1]]
                            if name == "down":
                                if step[2] == 0 and kind == "attn":
                                    pe.wait_ge(proj_kept, block)
                                down_quarter(s0 + step[1], K0 + g, step[2], banks)
                            else:
                                if kind == "attn" and K0 + g - 2 >= K0 and step[2] == 0:
                                    pe.wait_ge(y_added, 8 * (K0 + max(g - 2, 0)) + FREE_AT_START)
                                projected(s0 + step[1], name, kind, step[2], block, g)
                                block += step[2] % 2
                        elif step[0] == "scores":
                            group = attention_unit(step[1])[0] // 4
                            scores(step[1], first + [4, 6, 12, 18][group])
                        elif step[0] == "turn_probs":
                            turn_probs(step[1], K0 + attention_unit(step[1])[0] // 4)
                        elif step[0] == "values":
                            weigh_values(step[1])
                        elif step[0] == "level":
                            level_products(step[1], step[2], first + 8 * step[1] + 4)
                        elif step[0] == "turn_keys":
                            turn_keys(step[1])
                        elif step[0] == "updates":
                            updates(step[1], first + 8 * step[1] + 8)
                        elif step[0] == "outputs":
                            outputs(step[1])
                        elif kind == "attn":
                            pe.wait_ge(head_kept, 4 * step[1] + 4)
                            pe.wait_ge(probs_t_act, [4, 8, 16, 24][step[1]])
                            pe.wait_ge(probs_t_dve, two_bank_units([4, 8, 16, 24][step[1]]))
                            turn_out(att_out, 4)
                        else:
                            pe.wait_ge(normed_ready, step[1] + 1)
                            turn_out(normed, 2)
                    for t in range(NT):
                        down_quarter(s0 + len(slabs) - 1, K0 + 3, t, bank[4:8])
                if n < last_phase:
                    for t in range(NT):
                        pe.wait_ge(ln_done, NT * n + t + 1)
                        turn(n + 1, t)


_INS = ["x", "ffn_w1", "ffn_w3", "ffn_w2", "ln_g", "ln_b", "attn_w_in", "attn_sinks", "attn_w_out",
        "hgrn_w_in", "hgrn_norm_g", "hgrn_w_out", "hgrn_lower_bounds"]


def kernel(**inputs):
    import concourse.bacc as bacc
    from concourse.bass_utils import run_bass_kernel_spmd

    nc = bacc.Bacc("TRN2", target_bir_lowering=False, num_devices=1)
    arrays, args = {}, []
    for name in _INS:
        a = np.ascontiguousarray(inputs[name])
        arrays[f"in_{name}"] = a
        args.append(nc.dram_tensor(f"in_{name}", a.shape, mybir.dt.from_np(a.dtype), kind="ExternalInput").ap())
    args.append(nc.dram_tensor("out_x", (1, T, D), F32, kind="ExternalOutput").ap())
    build_trunk(nc, *args)
    return run_bass_kernel_spmd(nc, [arrays], core_ids=[0]).results[0]["out_x"]
```

```python
import numpy as np
import concourse.bass as bass
from concourse import mybir
from contextlib import ExitStack

F32 = mybir.dt.float32
F32R = mybir.dt.float32r
I32 = mybir.dt.int32
ALU = mybir.AluOpType
ACT = mybir.ActivationFunctionType
AX = mybir.AxisListType

P = 128
D = 1024
T = 512
DFF = 2816
NT = T // P
DC = D // P
GW = 256
NG = DFF // GW
SLAB = 2048
RING = 3
HALF = D // 2
ALPHA = 4.0 ** 0.25
LN_EPS = 1e-5 / (ALPHA * ALPHA)
RMS_EPS = 1e-6
LEVELS = [1, 2, 4, 8, 16, 32, 64]
MASK_STEPS = 1 + 2 * len(LEVELS)
TABLE_STEPS = 4 * 3 + 4 * 2
BLOCKS = 18
ARENA = 15360
FREE_AT_START = 4
HD = 64
SCALE = HD ** -0.5
SLOPES = [2.0 ** (-8.0 * (i + 1) / 16) for i in range(16)]
WINDOW = 128
FAR = 1.0e30
CH = 128

PHASES = [("ffn", (0, 0), (0, 0), 0.5), ("attn", 0, (0, 1), 1.0), ("ffn", (0, 1), (0, 2), 0.5),
          ("ffn", (1, 0), (1, 0), 0.5), ("hgrn", 0, (1, 1), 1.0), ("ffn", (1, 1), (1, 2), 0.5)]
SIZES = {"ffn": (3 * NG, NG), "attn": (13, 4), "hgrn": (20, 4)}


def layout(phases):
    out, s, k = [], 0, 0
    for ph in phases:
        out.append((s, k))
        s += SIZES[ph[0]][0]
        k += SIZES[ph[0]][1]
    return out, s


HGRN_PART = {"q": 0, "f": 1, "v": 2, "g": 3}
MIXER_SLABS = {
    "attn": ([("kv", 0), ("q", 0)],
             [[("q", 1), ("kb", 2)], [("q", 2), ("down", 0)],
              [("vb", 2), ("kb", 3), ("q", 3), ("down", 1)], [("vb", 3), ("down", 2)]]),
    "hgrn": ([("f", 0), ("q", 0)],
             [[("g", 0), ("v", 0), ("f", 1), ("q", 1)], [("g", 1), ("v", 1), ("f", 2), ("q", 2), ("down", 0)],
              [("g", 2), ("v", 2), ("f", 3), ("q", 3), ("down", 1)], [("g", 3), ("v", 3), ("down", 2)]]),
}
UNITS = [0, 4, 8, 16, 24]


def mixer_slabs(kind):
    first, between = MIXER_SLABS[kind]
    return first + [x for names in between for x in names] + [("down", 3)]


def blocks_until(kind, name, group):
    slabs = mixer_slabs(kind)
    return 2 * sum(x[0] != "down" for x in slabs[:slabs.index((name, group)) + 1])


def mixer_schedule(kind):
    steps, at = [], 2
    for g in range(4):
        fill = []
        for name, _ in MIXER_SLABS[kind][1][g]:
            fill += [("quarter", at, c) for c in range(4)]
            at += 1
        own = []
        if kind == "attn":
            a, b = UNITS[g], UNITS[g + 1]
            if g == 0:
                own += [("scores", 0), ("scores", 1)]
            if g >= 2:
                steps += fill[:4]
                fill = fill[4:]
            for u in range(a, b):
                own += [("turn_probs", u)] + ([("scores", u + 2)] if u + 2 < b else []) + [None, ("values", u), None]
            if g < 3:
                own += [("scores", b), ("scores", b + 1)]
            own.append(("turn_out", g))
            tail = []
        else:
            own = [x for a in range(0 if g == 0 else 2, 8) for x in (("level", g, a), None)]
            own += [("turn_keys", g), None, ("updates", g), None]
            tail = fill[-4:] if g else []
            fill = fill[:-4] if g else fill
        gaps, put, seen = own.count(None), 0, 0
        for step in own:
            if step is not None:
                if step[0] == "updates":
                    steps += fill[put:8]
                    put = max(put, 8)
                steps.append(step)
                continue
            seen += 1
            upto = max(put, len(fill) * seen // gaps)
            steps += fill[put:upto]
            put = upto
        if kind == "hgrn":
            steps.append(("outputs", g))
            steps += tail[:2]
            if g < 3:
                steps.append(("level", g + 1, 0))
            steps += tail[2:]
            if g < 3:
                steps.append(("level", g + 1, 1))
            steps.append(("turn_out", g))
    return steps


SWA_UNIT = ([(0, [0]), (1, [0, 1]), (2, [1, 2]), (3, [2, 3])], P)
MOBA_UNITS = [([(0, [0]), (2, [0, 1, 2]), (1, [0, 1])], 0), ([(3, [0, 1, 2, 3])], 0)]


def attention_unit(u):
    if u < 8:
        return u, SWA_UNIT[0], SWA_UNIT[1], True
    return 8 + (u - 8) // 2, *MOBA_UNITS[u % 2], u % 2 == 1


def decay_at(m):
    return 2 * T - 4 * T // m


def two_bank_units(u):
    return min(u, 8) + (max(u - 8, 0) + 1) // 2


def build_trunk(nc, x_in, w1, w3, w2, ln_g, ln_b, aw_in, sinks, aw_out, hw_in, hnorm, hw_out, lbs_in, out,
                phases=None):
    phases = PHASES if phases is None else phases
    bases, n_slabs = layout(phases)
    ffn_index = [sum(p[0] == "ffn" for p in phases[:n]) for n in range(len(phases))]
    last_phase = len(phases) - 1

    with ExitStack() as ctx:
        def sb(name, shape, dt=F32):
            return ctx.enter_context(nc.sbuf_tensor(name, shape, dt))

        def sem(name):
            return ctx.enter_context(nc.semaphore(name))

        raw = sb("raw", [P, RING, SLAB])
        w_hi = sb("w_hi", [P, RING, SLAB], F32R)
        w_lo = sb("w_lo", [P, RING, SLAB], F32R)
        x = sb("x", [P, NT, D])
        xt_hi = sb("xt_hi", [P, DC, T], F32R)
        xt_lo = sb("xt_lo", [P, DC, T], F32R)
        lng = sb("lng", [P, D])
        lnb = sb("lnb", [P, D])
        stats = sb("stats", [P, 2, 6])
        meanvar = sb("meanvar", [P, NT, 2])
        vareps = sb("vareps", [P, NT])
        rstd = sb("rstd", [P, NT])
        neghalf = sb("neghalf", [P, 8])
        ident = sb("ident", [P, P])
        gate = sb("gate", [P, 2, T])
        hid = sb("hid", [P, 2, T])
        h_hi = sb("h_hi", [P, 2, T], F32R)
        h_lo = sb("h_lo", [P, 2, T], F32R)
        psum = ctx.enter_context(nc.psum_tensor("psum", [P, 8 * T], F32))
        bank = [psum[:, i * T:(i + 1) * T] for i in range(8)]

        arena = sb("arena", [P, ARENA])
        cursor = [0]

        def cut(*shape):
            n = int(np.prod(shape))
            part = arena[:, cursor[0]:cursor[0] + n]
            cursor[0] += n
            assert cursor[0] <= ARENA
            if len(shape) == 2:
                return part.rearrange("p (a b) -> p a b", b=shape[1])
            if len(shape) == 3:
                return part.rearrange("p (a b c) -> p a b c", b=shape[1], c=shape[2])
            return part

        q_t = cut(2, 2, T)
        k_swa = cut(2, T)
        k_moba = cut(2, 2, T)
        v_swa = cut(NT, P)
        v_moba = cut(2, NT, GW)
        dist_swa = cut(7 * P)
        dist_moba = [cut(6 * P), cut(4 * P)]
        probs = cut(3, 7 * P)
        probs_t = cut(2, 7 * P)
        att_out = cut(NT, GW)
        cursor[0] = 0
        decay = cut(2, 2, T)
        qp = cut(2, 2, T)
        ks = cut(2, 2, T)
        values = cut(2, NT, GW)
        out_gate = cut(2, NT, GW)
        block_decay = cut(2 * T)
        squares = block_decay[:, 0:2 * T].rearrange("p (a b) -> p a b", b=P)
        within = cut(2, T)
        keys_tok = cut(2, T)
        normed = keys_tok.rearrange("p h n -> p (h n)").rearrange("p (t n) -> p t n", n=GW)
        state = cut(2, 3, P)
        sig_pos, sig_neg = gate, hid

        neg_max = sb("neg_max", [P, 3, 4])
        sums = sb("sums", [P, 4, 4])
        sink_part = sb("sink_part", [P, 4, 4])
        inv_sum = sb("inv_sum", [P, 4])
        total = sb("total", [P, 4])
        sink_b = sb("sink_b", [P, 8])
        neg_sink = sb("neg_sink", [P, 8])
        norm_b = sb("norm_b", [P, P])
        lb_rows = sb("lb_rows", [16, P])
        lb_t = sb("lb_t", [P, 2, 8])
        lb_m = sb("lb_m", [P, 8])
        lb_e = sb("lb_e", [P, 2, 8])
        lb_r = sb("lb_r", [P, 8])
        lower = sb("lower", [P, 8])
        span = sb("span", [P, 8])
        pair_mask_f = hid[:, 0, 0:7 * 64].rearrange("p (a b) -> p a b", b=64)
        pair_mask = sb("pair_mask", [P, 7, 64], mybir.dt.uint8)
        mean_sq = sb("mean_sq", [P, 8])
        rms_in = sb("rms_in", [P, 8])
        rms = sb("rms", [P, 8])

        x_loaded = sem("x_loaded")
        ident_zeroed = sem("ident_zeroed")
        consts_ready = sem("consts_ready")
        raw_landed = [sem(f"raw_landed{i}") for i in range(RING)]
        hi_ready = sem("hi_ready")
        lo_ready = sem("lo_ready")
        up1_done = sem("up1_done")
        up3_done = sem("up3_done")
        gate_done = sem("gate_done")
        hid_done = sem("hid_done")
        h_hi_done = sem("h_hi_done")
        h_lo_done = sem("h_lo_done")
        y_done = sem("y_done")
        y_added = sem("y_added")
        par_loaded = [sem(f"par_loaded{i}") for i in range(2)]
        stat_done = sem("stat_done")
        var_ready = sem("var_ready")
        rstd_ready = sem("rstd_ready")
        centred = sem("centred")
        ln_done = sem("ln_done")
        turn_done = sem("turn_done")
        xt_hi_done = sem("xt_hi_done")
        xt_lo_done = sem("xt_lo_done")
        out_stored = sem("out_stored")
        small_loaded = sem("small_loaded")
        lb_turned = sem("lb_turned")
        lb_exp = sem("lb_exp")
        set_up = sem("set_up")
        masks_step = sem("masks_step")
        proj_done = sem("proj_done")
        proj_kept = sem("proj_kept")
        kv_halves = sem("kv_halves")
        kv_copied = [sem(f"kv_copied{i}") for i in range(2)]
        scores_done = sem("scores_done")
        scores_kept = sem("scores_kept")
        max_ready = sem("max_ready")
        neg_max_ready = sem("neg_max_ready")
        exp_done = sem("exp_done")
        probs_turned = sem("probs_turned")
        probs_t_act = sem("probs_t_act")
        probs_t_dve = sem("probs_t_dve")
        head_done = sem("head_done")
        head_kept = sem("head_kept")
        out_turned = sem("out_turned")
        keys_ready = sem("keys_ready")
        level_done = sem("level_done")
        level_kept = sem("level_kept")
        level_step = sem("level_step")
        gate_normed = sem("gate_normed")
        keys_turned = sem("keys_turned")
        keys_tok_ready = sem("keys_tok_ready")
        updates_done = sem("updates_done")
        states_ready = sem("states_ready")
        outputs_done = sem("outputs_done")
        squares_done = sem("squares_done")
        rms_asked = sem("rms_asked")
        rms_ready = sem("rms_ready")
        normed_ready = sem("normed_ready")

        users = []
        for n, ph in enumerate(phases):
            K0 = bases[n][1]
            if ph[0] == "ffn":
                G0 = NG * ffn_index[n]
                users += [(up1_done, 2 * G0 + 2, 2), (up3_done, 2 * G0 + 2, 2)]
                for g in range(1, NG):
                    users += [(up1_done, 2 * (G0 + g) + 2, 2), (y_done, 8 * (K0 + g), 8),
                              (up3_done, 2 * (G0 + g) + 2, 2)]
                users.append((y_done, 8 * (K0 + NG), 8))
            else:
                first_block = BLOCKS * sum(p[0] != "ffn" for p in phases[:n])
                blocks = 0
                for name, g in mixer_slabs(ph[0]):
                    if name == "down":
                        users.append((y_done, 8 * (K0 + g + 1), 8))
                    else:
                        blocks += 2
                        users.append((proj_done, first_block + blocks, 2))

        LAST_BANKS = bank[4:8] + bank[0:4]

        mixers_before = [sum(p[0] != "ffn" for p in phases[:n]) for n in range(len(phases))]
        block_base = [BLOCKS * m for m in mixers_before]
        out_base = [8 * m for m in mixers_before]

        def proj_bank(s, j):
            return 2 * s + j if s < 2 else j

        block = ctx.enter_context(nc.Block())

        def upto(at, i, by=1):
            return at if i is None else at + by * i

        @block.sync
        def _(sp):
            def load_slab(s, src, i=None, view=None):
                if s >= RING or i is not None:
                    sp.wait_ge(lo_ready, upto(s - RING + 1, i, RING))
                dst = raw[:, s % RING, :]
                sp.dma_start(dst.rearrange("p (c n) -> p c n", n=src.shape[-1]), src).then_inc(raw_landed[s % RING], 16)

            def load_params(n):
                l, k = phases[n][2]
                if n:
                    sp.wait_ge(ln_done, NT * n)
                sp.dma_start(lng[:], ln_g[l, k:k + 1, :].broadcast_to([P, D])).then_inc(par_loaded[0], 16)
                sp.dma_start(lnb[:], ln_b[l, k:k + 1, :].broadcast_to([P, D])).then_inc(par_loaded[1], 16)

            def up_slab(w, g):
                return w[:, bass.ds(g * GW, GW)].rearrange("(c p) n -> p c n", p=P)

            def down_slab(w, g):
                return w[bass.ds(g * GW, GW), :].rearrange("(c p) n -> p c n", p=P)

            sp.dma_start(sink_b[:], sinks[0:1, :].broadcast_to([P, 8])).then_inc(small_loaded, 16)
            sp.dma_start(norm_b[:], hnorm[0:1, :].broadcast_to([P, P])).then_inc(small_loaded, 16)
            sp.dma_start(lb_rows[:], lbs_in.rearrange("l (h k) -> (l h) k", k=P)).then_inc(small_loaded, 16)
            if phases[0][0] != "ffn":
                for t in range(NT):
                    sp.dma_start(x[:, t, :], x_in[0, t * P:(t + 1) * P, :]).then_inc(x_loaded, 16)
            for n, (kind, wi, ln, _w) in enumerate(phases):
                s0 = bases[n][0]
                if kind == "ffn":
                    l, f = wi
                    a, b, c = w1[l, f], w3[l, f], w2[l, f]
                    load_slab(s0, up_slab(a, 0))
                    if n == 0:
                        for t in range(NT):
                            sp.dma_start(x[:, t, :], x_in[0, t * P:(t + 1) * P, :]).then_inc(x_loaded, 16)
                    load_slab(s0 + 1, up_slab(b, 0))
                    load_slab(s0 + 2, up_slab(a, 1))
                    load_params(n)
                    load_slab(s0 + 3, down_slab(c, 0))
                    load_slab(s0 + 4, up_slab(b, 1))
                    with sp.Fori(1, NG - 1) as i:
                        load_slab(s0 + 2, up_slab(a, i + 1), i)
                        load_slab(s0 + 3, down_slab(c, i), i)
                        load_slab(s0 + 4, up_slab(b, i + 1), i)
                    load_slab(s0 + 3 * NG - 1, down_slab(c, NG - 1))
                else:
                    for s, (name, g) in enumerate(mixer_slabs(kind)):
                        if s == RING:
                            load_params(n)
                        if kind == "attn":
                            swa, moba = 8 * HD, 8 * HD + 4 * HD
                            col = {"q": g * GW if g < 2 else moba + (g - 2) * GW, "kv": swa,
                                   "kb": moba + 512 + (g - 2) * GW, "vb": moba + 1024 + (g - 2) * GW}
                            src = down_slab(aw_out[0], g) if name == "down" else \
                                aw_in[0][:, col[name]:col[name] + GW].rearrange("(c p) n -> p c n", p=P)
                        else:
                            src = down_slab(hw_out[0], g) if name == "down" else \
                                hw_in[0][:, HGRN_PART[name] * D + g * GW:HGRN_PART[name] * D + (g + 1) * GW]\
                                .rearrange("(c p) n -> p c n", p=P)
                        load_slab(s0 + s, src)
            for t in range(NT):
                sp.wait_ge(ln_done, NT * last_phase + t + 1)
                sp.dma_start(out[0, t * P:(t + 1) * P, :], x[:, t, :]).then_inc(out_stored, 16)
            sp.wait_ge(out_stored, 16 * NT)

        @block.gpsimd
        def _(pool):
            pool.memset(neghalf[:], -0.5).then_inc(consts_ready, 1)
            pool.memset(ident[:], 0.0).then_inc(ident_zeroed, 1)
            pool.wait_ge(ident_zeroed, 1)
            pool.affine_select(out=ident[:], in_=ident[:], compare_op=ALU.not_equal, fill=1.0, base=0,
                               pattern=[[-1, P]], channel_multiplier=1).then_inc(consts_ready, 1)

            steps = [0]

            def then(op):
                op.then_inc(masks_step, 1)
                steps[0] += 1
                pool.wait_ge(masks_step, steps[0])

            def distances(table, tile, keys, window):
                n = len(keys) * P
                then(pool.iota(table, pattern=[[-1, n]], base=(tile - keys[0]) * P, channel_multiplier=1,
                               allow_small_or_imprecise_dtypes=True))
                then(pool.affine_select(out=table, in_=table, compare_op=ALU.is_ge, fill=FAR,
                                        base=(tile - keys[0]) * P, pattern=[[-1, n]], channel_multiplier=1))
                if window:
                    then(pool.affine_select(out=table, in_=table, compare_op=ALU.is_ge, fill=FAR,
                                            base=WINDOW - 1 - (tile - keys[0]) * P, pattern=[[1, n]],
                                            channel_multiplier=-1))

            def attention_tables():
                for table, (tiles, _) in [(dist_swa, SWA_UNIT), (dist_moba[0], MOBA_UNITS[0]), (dist_moba[1], MOBA_UNITS[1])]:
                    at = 0
                    for tile, keys in tiles:
                        distances(table[:, at:at + len(keys) * P], tile, keys, table is dist_swa)
                        at += len(keys) * P

            then(pool.memset(pair_mask_f, 1.0))
            for a, m in enumerate(LEVELS):
                view = pair_mask_f[:, a, :].rearrange("p (b e) -> p b e", e=m)
                then(pool.affine_select(out=view, in_=view, compare_op=ALU.is_ge, fill=0.0, base=0,
                                        pattern=[[-2 * m, 64 // m], [0, m]], channel_multiplier=1))
                then(pool.affine_select(out=view, in_=view, compare_op=ALU.is_ge, fill=0.0, base=m - 1,
                                        pattern=[[2 * m, 64 // m], [0, m]], channel_multiplier=-1))

            def low(s, i=None):
                pool.wait_ge(hi_ready, upto(s + 1, i, RING))
                pool.tensor_tensor(w_lo[:, s % RING, :], raw[:, s % RING, :], w_hi[:, s % RING, :].bitcast(F32),
                                   ALU.subtract).then_inc(lo_ready, 1)

            def norm_powers(n):
                for t in range(NT):
                    pool.wait_ge(var_ready, NT * n + t + 1)
                    pool.tensor_tensor(rstd[:, t:t + 1], vareps[:, t:t + 1], neghalf[:, 0:1],
                                       ALU.pow).then_inc(rstd_ready, 1)

            for s in range(min(RING, n_slabs)):
                low(s)
            for n, (kind, wi, ln, _w) in enumerate(phases):
                s0 = bases[n][0]
                if kind == "ffn":
                    with pool.Fori(0, NG - 1) as i:
                        for j in range(RING):
                            low(s0 + RING + j, i)
                    if n < last_phase:
                        for s in range(s0 + 3 * NG, s0 + 3 * NG + 2):
                            low(s)
                    norm_powers(n)
                    if n < last_phase:
                        low(s0 + 3 * NG + 2)
                else:
                    slabs, plan = mixer_slabs(kind), mixer_schedule(kind)
                    if kind == "attn":
                        attention_tables()
                    low(s0 + RING)
                    low(s0 + RING + 1)
                    for step in plan:
                        if step[0] == "quarter" and step[2] == 3 and s0 + step[1] + RING < n_slabs:
                            low(s0 + step[1] + RING)
                        if step[0] == "quarter" and step[2] == 3 and slabs[step[1]][0] == "g":
                            g = slabs[step[1]][1]
                            pool.wait_ge(small_loaded, 48)
                            pool.wait_ge(proj_kept, block_base[n] + blocks_until(kind, "g", g))
                            view = out_gate[:, g % 2].rearrange("p t (h n) -> p (t h) n", n=P)
                            pool.tensor_tensor(view, view, norm_b[:, None, :].broadcast_to([P, 8, P]),
                                               ALU.mult).then_inc(gate_normed, 1)
                        if step[0] == "outputs":
                            pool.wait_ge(rms_asked, step[1] + 1)
                            pool.tensor_tensor(rms[:], rms_in[:], neghalf[:], ALU.pow).then_inc(rms_ready, 1)
                    norm_powers(n)
                    if s0 + len(slabs) + 2 < n_slabs:
                        low(s0 + len(slabs) + 2)

        @block.scalar
        def _(act):
            def high(s, i=None):
                act.wait_ge(raw_landed[s % RING], upto(16 * (s // RING + 1), i, 16))
                if s >= RING:
                    used, count, by = users[s - RING]
                    act.wait_ge(used, upto(count, i, by))
                act.activation(w_hi[:, s % RING, :], raw[:, s % RING, :], ACT.Copy).then_inc(hi_ready, 1)

            def turn_high(turn, t):
                for b in range(2):
                    act.wait_ge(turn_done, 8 * turn + 2 * t + b + 1)
                    act.activation(xt_hi[:, 4 * b:4 * b + 4, t * P:(t + 1) * P],
                                   bank[4 + 2 * (t % 2) + b].rearrange("p (c n) -> p c n", n=P),
                                   ACT.Copy).then_inc(xt_hi_done, 1)

            def gates(G, i=None):
                for j in range(2):
                    act.wait_ge(up1_done, upto(2 * G + j + 1, i, 2))
                    if G:
                        act.wait_ge(hid_done, upto(2 * (G - 1) + j + 1, i, 2))
                    act.activation(gate[:, j, :], bank[j][:], ACT.Silu).then_inc(gate_done, 1)

            def hid_high(G, K, i=None):
                for j in range(2):
                    act.wait_ge(hid_done, upto(2 * G + j + 1, i, 2))
                    if K:
                        act.wait_ge(y_done, upto(8 * K, i, 8))
                    act.activation(h_hi[:, j, :], hid[:, j, :], ACT.Copy).then_inc(h_hi_done, 1)

            high(0)
            high(1)
            act.wait_ge(lb_turned, 1)
            act.activation(lb_t[:].rearrange("p l h -> p (l h)"), bank[3][:, 0:16], ACT.Copy).then_inc(lb_exp, 1)
            act.wait_ge(set_up, 2)
            act.activation(lb_e[:], lb_t[:], ACT.Exp).then_inc(lb_exp, 1)

            def turn_all_high(turn, spare_slab):
                turn_high(turn, 0)
                turn_high(turn, 1)
                high(spare_slab)
                turn_high(turn, 2)
                turn_high(turn, 3)

            turn_all_high(0, 2)

            def keep_block(kind, slabs, s, j, block):
                name, g = slabs[s]
                src = bank[proj_bank(s, j)]
                two_tiles = src.rearrange("p (t n) -> p t n", n=GW)
                act.wait_ge(proj_done, block + 1)
                if name == "q" and kind == "attn":
                    op = act.activation(q_t[:, g % 2, j, :], src, ACT.Copy, scale=SCALE)
                elif name == "kv" and j == 0:
                    act.activation(k_swa[0:HD, 0, :], src[0:HD, :], ACT.Copy).then_inc(kv_halves, 1)
                    op = act.activation(k_swa[HD:P, 1, :], src[HD:P, :], ACT.Copy)
                elif name == "kv":
                    op = act.activation(v_swa, src.rearrange("p (t n) -> p t n", n=P), ACT.Copy)
                elif name == "kb":
                    op = act.activation(k_moba[:, g % 2, j, :], src, ACT.Copy)
                elif name == "vb":
                    op = act.activation(v_moba[:, g % 2, 2 * j:2 * j + 2, :], two_tiles, ACT.Copy)
                elif name == "f":
                    if g:
                        act.wait_ge(keys_ready, 2 * (g - 1) + j + 1)
                    act.activation(sig_pos[:, j, :], src, ACT.Sigmoid)
                    op = act.activation(sig_neg[:, j, :], src, ACT.Sigmoid, scale=-1.0)
                elif name == "q":
                    op = act.activation(qp[:, g % 2, j, :], src, ACT.Silu)
                elif name == "g":
                    op = act.activation(out_gate[:, g % 2, 2 * j:2 * j + 2, :], two_tiles, ACT.Silu)
                else:
                    op = act.activation(values[:, g % 2, 2 * j:2 * j + 2, :], two_tiles, ACT.Copy)
                op.then_inc(proj_kept, 1)
                if name == "kv" and j == 0:
                    act.wait_ge(kv_halves, 1)
                    act.dma_start(k_swa[HD:P, 0, :], k_swa[0:HD, 0, :]).then_inc(kv_copied[0], 16)
                    act.wait_ge(proj_kept, block + 1)
                    act.dma_start(k_swa[0:HD, 1, :], k_swa[HD:P, 1, :]).then_inc(kv_copied[1], 16)

            def exponentials(u):
                head, tiles, _, _ = attention_unit(u)
                act.wait_ge(neg_max_ready, u + 1)
                at = 0
                for n_, (tile, keys) in enumerate(tiles):
                    part = probs[:, u % 3, at:at + len(keys) * P]
                    op = act.activation(part, part, ACT.Exp, bias=neg_max[:, u % 3, n_:n_ + 1],
                                        accum_out=sums[:, head % 4, tile:tile + 1])
                    at += len(keys) * P
                if head < 8:
                    op = act.activation(sink_part[:, head % 4, :], neg_max[:, u % 3, :], ACT.Exp,
                                        bias=sink_b[:, head:head + 1])
                op.then_inc(exp_done, 1)

            def probs_first_bank(u):
                act.wait_ge(probs_turned, u + 1)
                act.activation(probs_t[:, u % 2, 0:4 * P], bank[4], ACT.Copy).then_inc(probs_t_act, 1)

            def turned_out_high(outs, K):
                for j in range(2):
                    act.wait_ge(out_turned, outs + j + 1)
                    if K:
                        act.wait_ge(y_done, 8 * K)
                    act.activation(h_hi[:, j, :], bank[4 + j], ACT.Copy).then_inc(h_hi_done, 1)
            for n, (kind, wi, ln, _w) in enumerate(phases):
                s0, K0 = bases[n]
                if kind == "ffn":
                    G0 = NG * ffn_index[n]
                    gates(G0)
                    high(s0 + 3)
                    hid_high(G0, K0)
                    high(s0 + 4)
                    with act.Fori(0, NG - 2) as i:
                        gates(G0 + 1, i)
                        high(s0 + 5, i)
                        high(s0 + 6, i)
                        hid_high(G0 + 1, K0 + 1, i)
                        high(s0 + 7, i)
                    gates(G0 + NG - 1)
                    high(s0 + 3 * NG - 1)
                    if n < last_phase:
                        high(s0 + 3 * NG)
                    hid_high(G0 + NG - 1, K0 + NG - 1)
                    if n < last_phase:
                        high(s0 + 3 * NG + 1)
                else:
                    slabs, plan = mixer_slabs(kind), mixer_schedule(kind)
                    block, outs = block_base[n], out_base[n]
                    for s in range(2):
                        for j in range(2):
                            keep_block(kind, slabs, s, j, block)
                            block += 1
                        high(s0 + s + RING)
                    for step in plan:
                        if step[0] == "quarter":
                            name = slabs[step[1]][0]
                            if name != "down" and step[2] % 2 == 1:
                                keep_block(kind, slabs, step[1], step[2] // 2, block)
                                block += 1
                            if step[2] == 3 and s0 + step[1] + RING < n_slabs:
                                high(s0 + step[1] + RING)
                        elif step[0] == "scores":
                            exponentials(step[1])
                        elif step[0] == "turn_probs":
                            probs_first_bank(step[1])
                        elif step[0] == "turn_keys":
                            for h in range(2):
                                act.wait_ge(keys_turned, 2 * step[1] + h + 1)
                                act.activation(keys_tok[:, h, :], bank[4 + h], ACT.Copy).then_inc(keys_tok_ready, 1)
                        elif step[0] == "outputs":
                            for b in range(2):
                                act.wait_ge(outputs_done, 2 * step[1] + b + 1)
                                act.activation(squares[:, 4 * b:4 * b + 4, :],
                                               bank[4 + b].rearrange("p (a n) -> p a n", n=P),
                                               ACT.Square).then_inc(squares_done, 1)
                        elif step[0] == "turn_out":
                            turned_out_high(outs + 2 * step[1], K0 + step[1])
                if n < last_phase:
                    turn_all_high(n + 1, bases[n + 1][0] + 2)

        @block.vector
        def _(dve):
            def turn_low(turn, t):
                for b in range(2):
                    dve.wait_ge(xt_hi_done, 8 * turn + 2 * t + b + 1)
                    part = (slice(None), slice(4 * b, 4 * b + 4), slice(t * P, (t + 1) * P))
                    dve.tensor_tensor(xt_lo[part], bank[4 + 2 * (t % 2) + b].rearrange("p (c n) -> p c n", n=P),
                                      xt_hi[part].bitcast(F32), ALU.subtract).then_inc(xt_lo_done, 1)

            def hiddens(G, i=None):
                for j in range(2):
                    dve.wait_ge(gate_done, upto(2 * G + j + 1, i, 2))
                    dve.wait_ge(up3_done, upto(2 * G + j + 1, i, 2))
                    dve.tensor_tensor(hid[:, j, :], bank[2 + j][:], gate[:, j, :], ALU.mult).then_inc(hid_done, 1)

            def hid_low(K, i=None):
                for j in range(2):
                    dve.wait_ge(h_hi_done, upto(2 * K + j + 1, i, 2))
                    dve.tensor_tensor(h_lo[:, j, :], hid[:, j, :], h_hi[:, j, :].bitcast(F32),
                                      ALU.subtract).then_inc(h_lo_done, 1)

            def add_piece(K, k, weight, banks, i=None):
                t, half = divmod(k, 2)
                dve.wait_ge(y_done, upto(8 * K + k + 1, i, 8))
                part = x[:, t, half * HALF:(half + 1) * HALF]
                dve.scalar_tensor_tensor(out=part, in0=banks[k % len(banks)][:], scalar=weight / ALPHA, in1=part,
                                         op0=ALU.mult, op1=ALU.add).then_inc(y_added, 1)

            chain = [0]

            def then(op):
                op.then_inc(stat_done, 1)
                chain[0] += 1
                dve.wait_ge(stat_done, chain[0])

            def logits(u):
                head, tiles, col, _ = attention_unit(u)
                width = sum(len(keys) for _, keys in tiles) * P
                table = dist_swa if u < 8 else dist_moba[u % 2]
                dve.wait_ge(scores_done, u + 1)
                if u >= 3:
                    dve.wait_ge(probs_turned, u - 2)
                lg = probs[:, u % 3, 0:width]
                dve.scalar_tensor_tensor(out=lg, in0=table, scalar=-SLOPES[head],
                                         in1=psum[:, 2 * T + col:2 * T + col + width],
                                         op0=ALU.mult, op1=ALU.add).then_inc(scores_kept, 1)
                dve.wait_ge(scores_kept, u + 1)
                at = 0
                for n_, (tile, keys) in enumerate(tiles):
                    op = dve.tensor_reduce(neg_max[:, u % 3, n_:n_ + 1], probs[:, u % 3, at:at + len(keys) * P],
                                           AX.X, ALU.max, negate=True)
                    at += len(keys) * P
                if head < 8:
                    op.then_inc(max_ready, 1)
                    dve.wait_ge(max_ready, u + 1)
                    op = dve.tensor_scalar(neg_max[:, u % 3, :], neg_max[:, u % 3, :], neg_sink[:, head:head + 1],
                                           None, ALU.min)
                op.then_inc(neg_max_ready, 1)

            def probs_second_bank(u):
                blocks = sum(len(keys) for _, keys in attention_unit(u)[1])
                if blocks > 4:
                    dve.wait_ge(probs_turned, u + 1)
                    dve.tensor_copy(probs_t[:, u % 2, 4 * P:blocks * P],
                                    bank[5][:, 0:(blocks - 4) * P]).then_inc(probs_t_dve, 1)

            def keep_head(u):
                head, _, _, ends = attention_unit(u)
                if not ends:
                    return
                dve.wait_ge(head_done, head + 1)
                dve.wait_ge(exp_done, u + 1)
                sum_ = sums[:, head % 4, :]
                if head < 8:
                    then(dve.tensor_tensor(total[:], sum_, sink_part[:, head % 4, :], ALU.add))
                    sum_ = total[:]
                then(dve.reciprocal(inv_sum[:], sum_))
                dve.tensor_tensor(att_out[:, :, (head % 4) * HD:(head % 4 + 1) * HD],
                                  bank[6 + head % 2][:, 0:NT * HD].rearrange("p (t n) -> p t n", n=HD),
                                  inv_sum[:, :, None].broadcast_to([P, NT, HD]), ALU.mult).then_inc(head_kept, 1)

            def decays_and_keys(g, j, first_block):
                head = 2 * g + j
                dve.wait_ge(proj_kept, first_block + blocks_until("hgrn", "f", g) - 1 + j)
                dve.tensor_scalar(decay[:, g % 2, j, :], sig_pos[:, j, :], span[:, head:head + 1],
                                  lower[:, head:head + 1], ALU.mult, ALU.add)
                dve.tensor_scalar(ks[:, g % 2, j, :], sig_neg[:, j, :], span[:, head:head + 1], None,
                                  ALU.mult).then_inc(keys_ready, 1)

            def level(g, a):
                q_, k_, par = qp[:, g % 2], ks[:, g % 2], g % 2
                dve.wait_ge(level_done, 8 * g + a + 1)
                if a == 0:
                    for h in range(2):
                        dve.tensor_tensor(within[:, h, :].rearrange("p (c t) -> p c t", t=P),
                                          bank[2 + h].rearrange("p (c t) -> p c t", t=P),
                                          ident[:, None, :].broadcast_to([P, 4, P]), ALU.mult)
                    dve.tensor_tensor(q_, q_, decay[:, par], ALU.mult).then_inc(level_kept, 1)
                    dve.wait_ge(level_kept, 8 * g + 1)
                    return
                m = LEVELS[a - 1]
                n_ = T // (2 * m)
                pairs = "p h (b two e) -> p (h b) two e"
                at = within[:].rearrange(pairs, two=2, e=m)[:, :, 1, :]
                dst = at.rearrange("p (x b) e -> p x b e", b=64 // m)
                dve.copy_predicated(dst, pair_mask[:, a - 1, :].rearrange("p (b e) -> p b e", e=m)[:, None, :, :]
                                    .broadcast_to([P, 8, 64 // m, m]),
                                    bank[2 + a % 2].rearrange("p (x b e) -> p x b e", b=64 // m, e=m))
                old = decay[:, par].rearrange("p h t -> p (h t)") if m == 1 else \
                    block_decay[:, decay_at(m):decay_at(m) + 2 * T // m]
                old = old.rearrange("p (b two) -> p b two", two=2)
                qv = q_.rearrange(pairs, two=2, e=m)[:, :, 1, :]
                kv = k_.rearrange(pairs, two=2, e=m)[:, :, 0, :]
                dve.tensor_tensor(qv, qv, old[:, :, 0:1].broadcast_to([P, 2 * n_, m]), ALU.mult)
                dve.tensor_tensor(kv, kv, old[:, :, 1:2].broadcast_to([P, 2 * n_, m]), ALU.mult)
                dve.tensor_tensor(block_decay[:, decay_at(2 * m):decay_at(2 * m) + 2 * n_], old[:, :, 0],
                                  old[:, :, 1], ALU.mult).then_inc(level_kept, 1)
                dve.wait_ge(level_kept, 8 * g + a + 1)

            def states(g):
                dve.wait_ge(updates_done, g + 1)
                for c in range(3):
                    for h in range(2):
                        upd = bank[2 + h][:, c * P:(c + 1) * P]
                        if c == 0:
                            op = dve.tensor_copy(state[:, h, 0, :], upd)
                        else:
                            whole = block_decay[:, decay_at(P) + 4 * h + c:decay_at(P) + 4 * h + c + 1]
                            op = dve.scalar_tensor_tensor(out=state[:, h, c, :], in0=state[:, h, c - 1, :],
                                                          scalar=whole, in1=upd, op0=ALU.mult, op1=ALU.add)
                    if c < 2:
                        then(op)
                op.then_inc(states_ready, 1)

            def norm_outputs(g):
                dve.wait_ge(squares_done, 2 * g + 2)
                then(dve.tensor_reduce(mean_sq[:], squares, AX.X, ALU.add))
                dve.tensor_scalar(rms_in[:], mean_sq[:], 1.0 / P, RMS_EPS, ALU.mult, ALU.add).then_inc(rms_asked, 1)
                dve.wait_ge(rms_ready, g + 1)
                dve.wait_ge(gate_normed, g + 1)
                dve.wait_ge(keys_tok_ready, 2 * g + 2)
                for t in range(NT):
                    for h in range(2):
                        op = dve.scalar_tensor_tensor(
                            out=normed[:, t, h * P:(h + 1) * P],
                            in0=bank[4 + t // 2][:, (t % 2) * GW + h * P:(t % 2) * GW + (h + 1) * P],
                            scalar=rms[:, 2 * t + h:2 * t + h + 1], in1=out_gate[:, g % 2, t, h * P:(h + 1) * P],
                            op0=ALU.mult, op1=ALU.mult)
                op.then_inc(normed_ready, 1)

            def last_down_and_norm(n, K, weight):
                def sums_of(t):
                    for k in (2 * t, 2 * t + 1):
                        add_piece(K, k, weight, LAST_BANKS)
                    dve.wait_ge(y_added, FREE_AT_START + 8 * K + 2 * t + 1)
                    dve.bn_stats(stats[:, 0, :], x[:, t, 0:HALF])
                    dve.wait_ge(y_added, FREE_AT_START + 8 * K + 2 * t + 2)
                    then(dve.bn_stats(stats[:, 1, :], x[:, t, HALF:D]))
                    then(dve.bn_aggr(meanvar[:, t, :], stats[:, :, :]))
                    dve.tensor_scalar(vareps[:, t:t + 1], meanvar[:, t, 1:2], LN_EPS, None,
                                      ALU.add).then_inc(var_ready, 1)

                def normalise(t):
                    if t == 0:
                        dve.wait_ge(par_loaded[0], 16 * (n + 1))
                        dve.wait_ge(par_loaded[1], 16 * (n + 1))
                    dve.scalar_tensor_tensor(out=x[:, t, :], in0=x[:, t, :], scalar=meanvar[:, t, 0:1],
                                             in1=lng[:], op0=ALU.subtract, op1=ALU.mult).then_inc(centred, 1)
                    dve.wait_ge(centred, NT * n + t + 1)
                    dve.wait_ge(rstd_ready, NT * n + t + 1)
                    dve.scalar_tensor_tensor(out=x[:, t, :], in0=x[:, t, :], scalar=rstd[:, t:t + 1],
                                             in1=lnb[:], op0=ALU.mult, op1=ALU.add).then_inc(ln_done, 1)

                def low_(t):
                    if n < last_phase:
                        turn_low(n + 1, t)

                sums_of(0)
                sums_of(1)
                normalise(0)
                normalise(1)
                low_(0)
                sums_of(2)
                low_(1)
                sums_of(3)
                normalise(2)
                normalise(3)
                low_(2)
                low_(3)

            dve.memset(stats[:], 0.0).then_inc(y_added, FREE_AT_START)
            dve.wait_ge(lb_exp, 1)
            dve.tensor_tensor(lb_m[:], lb_t[:, 0, :], lb_t[:, 1, :], ALU.max).then_inc(set_up, 1)
            dve.wait_ge(set_up, 1)
            dve.tensor_tensor(lb_t[:], lb_t[:], lb_m[:, None, :].broadcast_to([P, 2, 8]),
                              ALU.subtract).then_inc(set_up, 1)
            dve.wait_ge(lb_exp, 2)
            dve.tensor_tensor(lb_m[:], lb_e[:, 0, :], lb_e[:, 1, :], ALU.add).then_inc(set_up, 1)
            dve.wait_ge(set_up, 3)
            dve.reciprocal(lb_r[:], lb_m[:]).then_inc(set_up, 1)
            dve.wait_ge(set_up, 4)
            dve.tensor_tensor(lower[:], lb_e[:, 1, :], lb_r[:], ALU.mult)
            dve.tensor_tensor(span[:], lb_e[:, 0, :], lb_r[:], ALU.mult)
            dve.wait_ge(small_loaded, 48)
            dve.tensor_scalar(neg_sink[:], sink_b[:], -1.0, None, ALU.mult)
            dve.wait_ge(masks_step, MASK_STEPS)
            dve.tensor_copy(pair_mask[:], pair_mask_f).then_inc(set_up, 1)
            dve.wait_ge(set_up, 5)
            for t in range(NT):
                turn_low(0, t)
            for n, (kind, wi, ln, weight) in enumerate(phases):
                s0, K0 = bases[n]
                if kind == "ffn":
                    G0 = NG * ffn_index[n]
                    hiddens(G0)
                    hid_low(K0)
                    with dve.Fori(0, NG - 1) as i:
                        for k in range(8):
                            add_piece(K0, k, weight, bank[4:8], i)
                        hiddens(G0 + 1, i)
                        hid_low(K0 + 1, i)
                    last_down_and_norm(n, K0 + NG - 1, weight)
                else:
                    slabs, plan = mixer_slabs(kind), mixer_schedule(kind)
                    banks = bank[0:2] if kind == "attn" else bank[6:8]
                    outs = out_base[n]
                    if kind == "attn":
                        dve.wait_ge(masks_step, MASK_STEPS + TABLE_STEPS)
                    if kind == "hgrn":
                        decays_and_keys(0, 0, block_base[n])
                        decays_and_keys(0, 1, block_base[n])
                    for step in plan:
                        if step[0] == "quarter":
                            name, g = slabs[step[1]]
                            if name == "down":
                                add_piece(K0 + g, 2 * step[2], weight, banks)
                                add_piece(K0 + g, 2 * step[2] + 1, weight, banks)
                            if name == "f" and step[2] % 2 == 1:
                                decays_and_keys(g, step[2] // 2, block_base[n])
                        elif step[0] == "scores":
                            logits(step[1])
                        elif step[0] == "turn_probs":
                            probs_second_bank(step[1])
                        elif step[0] == "values":
                            keep_head(step[1])
                        elif step[0] == "level":
                            level(step[1], step[2])
                        elif step[0] == "updates":
                            states(step[1])
                        elif step[0] == "outputs":
                            norm_outputs(step[1])
                        elif step[0] == "turn_out":
                            for j in range(2):
                                dve.wait_ge(h_hi_done, 2 * (K0 + step[1]) + j + 1)
                                dve.tensor_tensor(h_lo[:, j, :], bank[4 + j],
                                                  h_hi[:, j, :].bitcast(F32), ALU.subtract).then_inc(h_lo_done, 1)
                    last_down_and_norm(n, K0 + 3, weight)

        @block.tensor
        def _(pe):
            def three(out_, w, xs, first, last):
                pe.matmul(out_, w[0], xs[0], start=first, stop=False)
                pe.matmul(out_, w[0], xs[1], start=False, stop=False)
                return pe.matmul(out_, w[1], xs[0], start=False, stop=last)

            def features(out_, slot, j, tok):
                for c in range(DC):
                    cols = slice(c * GW + j * P, c * GW + (j + 1) * P)
                    mm = three(out_, (w_hi[:, slot, cols], w_lo[:, slot, cols]),
                               (xt_hi[:, c, tok], xt_lo[:, c, tok]), c == 0, c == DC - 1)
                return mm

            def turn(turn_no, t):
                if t >= 2:
                    pe.wait_ge(xt_lo_done, 8 * turn_no + 2 * (t - 1))
                if turn_no:
                    pe.wait_ge(ln_done, NT * (turn_no - 1) + t + 1)
                else:
                    pe.wait_ge(x_loaded, 16 * NT)
                for b in range(2):
                    for c in range(4):
                        mm = pe.transpose(bank[4 + 2 * (t % 2) + b][:, c * P:(c + 1) * P],
                                          x[:, t, (4 * b + c) * P:(4 * b + c + 1) * P], ident[:])
                    mm.then_inc(turn_done, 1)

            def up(s, G, done, freed, b0, i):
                pe.wait_ge(lo_ready, upto(s + 1, i, RING))
                for j in range(2):
                    pe.wait_ge(freed, upto(2 * G - 1 + j, i, 2))
                    features(bank[b0 + j], s % RING, j, slice(0, T)).then_inc(done, 1)

            def begin(n, first_two):
                K = bases[n][1]
                turn(n, 0)
                turn(n, 1)
                pe.wait_ge(lo_ready, bases[n][0] + 1)
                if n:
                    pe.wait_ge(y_added, FREE_AT_START + 8 * K - 2)
                pe.wait_ge(xt_lo_done, 8 * n + 4)
                first_two(0, 0)
                turn(n, 2)
                pe.wait_ge(lo_ready, bases[n][0] + 2)
                if n:
                    pe.wait_ge(y_added, FREE_AT_START + 8 * K)
                first_two(1, 0)
                turn(n, 3)
                pe.wait_ge(xt_lo_done, 8 * n + 8)
                first_two(0, 1)
                first_two(1, 1)

            def down(s, K, banks, i=None):
                for t in range(NT):
                    down_quarter(s, K, t, banks, i)

            def down_quarter(s, K, t, banks, i=None):
                slot = s % RING
                if t == 0:
                    pe.wait_ge(lo_ready, upto(s + 1, i, RING))
                    pe.wait_ge(h_lo_done, upto(2 * K + 2, i, 2))
                for k in (2 * t, 2 * t + 1):
                    half = k % 2
                    if len(banks) <= 4 or k < 4:
                        pe.wait_ge(y_added, upto(8 * K + k + 1 + FREE_AT_START - min(len(banks), 4), i, 8))
                    tok = slice(t * P, (t + 1) * P)
                    for c in range(2):
                        cols = slice(c * D + half * HALF, c * D + (half + 1) * HALF)
                        mm = three(banks[k % len(banks)][:], (h_hi[:, c, tok], h_lo[:, c, tok]),
                                   (w_hi[:, slot, cols], w_lo[:, slot, cols]), c == 0, c == 1)
                    mm.then_inc(y_done, 1)

            def token_tiles(out_, slot, tiles, n_, first_col):
                for t in tiles:
                    at = t * n_ % T
                    tok = slice(t * P, (t + 1) * P)
                    for c in range(DC):
                        cols = slice(c * GW + first_col, c * GW + first_col + n_)
                        mm = three(out_[:, at:at + n_], (xt_hi[:, c, tok], xt_lo[:, c, tok]),
                                   (w_hi[:, slot, cols], w_lo[:, slot, cols]), c == 0, c == DC - 1)
                return mm

            def mixer_first_two(s0, slabs):
                def first_two(s, half):
                    for j in range(2):
                        out_ = bank[proj_bank(s, j)]
                        if slabs[s][0] == "kv" and j == 1:
                            mm = token_tiles(out_, (s0 + s) % RING, [2 * half, 2 * half + 1], P, P)
                        else:
                            tok = slice(half * T // 2, (half + 1) * T // 2)
                            mm = features(out_[:, tok], (s0 + s) % RING, j, tok)
                        if half:
                            mm.then_inc(proj_done, 1)
                return first_two

            def ffn_first_two(s0):
                def first_two(s, half):
                    tok = slice(half * T // 2, (half + 1) * T // 2)
                    for j in range(2):
                        mm = features(bank[2 * s + j][:, tok], (s0 + s) % RING, j, tok)
                        if half:
                            mm.then_inc((up1_done, up3_done)[s], 1)
                return first_two

            def projected(s, name, quarter, block):
                slot = s % RING
                j, half = divmod(quarter, 2)
                if quarter == 0:
                    pe.wait_ge(lo_ready, s + 1)
                if half == 0:
                    pe.wait_ge(proj_kept, block - 1)
                out_ = bank[j]
                token_major = name in ("v", "g", "vb")
                if not token_major:
                    for c in range(4 * half, 4 * half + 4):
                        cols = slice(c * GW + j * P, c * GW + (j + 1) * P)
                        mm = three(out_, (w_hi[:, slot, cols], w_lo[:, slot, cols]),
                                   (xt_hi[:, c, :], xt_lo[:, c, :]), c == 0, c == DC - 1)
                else:
                    mm = token_tiles(out_, slot, [2 * j + half], GW, 0)
                if half == 1:
                    mm.then_inc(proj_done, 1)

            def scores(u, blocks_needed):
                head, tiles, col, _ = attention_unit(u)
                g = head // 4
                rows = slice((head % 2) * HD, (head % 2 + 1) * HD)
                if u:
                    pe.wait_ge(scores_kept, u)
                pe.wait_ge(proj_kept, blocks_needed)
                if u == 0:
                    pe.wait_ge(kv_copied[0], 16)
                    pe.wait_ge(kv_copied[1], 16)
                at = 2 * T + col
                for tile, keys in tiles:
                    kt = k_swa[rows, g, :] if head < 8 else k_moba[rows, g % 2, (head % 4) // 2, :]
                    mm = pe.matmul(psum[:, at:at + len(keys) * P],
                                   q_t[rows, g % 2, (head % 4) // 2, tile * P:(tile + 1) * P],
                                   kt[:, keys[0] * P:(keys[-1] + 1) * P], start=True, stop=True)
                    at += len(keys) * P
                mm.then_inc(scores_done, 1)

            def turn_probs(u, K):
                blocks = sum(len(keys) for _, keys in attention_unit(u)[1])
                pe.wait_ge(exp_done, u + 1)
                if u:
                    pe.wait_ge(probs_t_act, u)
                    pe.wait_ge(probs_t_dve, two_bank_units(u))
                pe.wait_ge(h_lo_done, 2 * K) if K else None
                for b in range(blocks):
                    mm = pe.transpose(psum[:, 4 * T + b * P:4 * T + (b + 1) * P],
                                      probs[:, u % 3, b * P:(b + 1) * P], ident[:])
                mm.then_inc(probs_turned, 1)

            def weigh_values(u, blocks_needed):
                head, tiles, _, ends = attention_unit(u)
                pe.wait_ge(proj_kept, blocks_needed)
                pe.wait_ge(probs_t_act, u + 1)
                pe.wait_ge(probs_t_dve, two_bank_units(u + 1))
                if head >= 2:
                    pe.wait_ge(head_kept, head - 1)
                b = 0
                for tile, keys in tiles:
                    for key in keys:
                        v_ = v_swa[:, key, (head // 4) * HD:(head // 4 + 1) * HD] if head < 8 else \
                            v_moba[:, (head // 4) % 2, key, (head % 4) * HD:(head % 4 + 1) * HD]
                        mm = pe.matmul(bank[6 + head % 2][:, tile * HD:(tile + 1) * HD],
                                       probs_t[:, u % 2, b * P:(b + 1) * P], v_,
                                       start=key == keys[0], stop=key == keys[-1])
                        b += 1
                if ends:
                    mm.then_inc(head_done, 1)

            def level_products(g, a, blocks_needed):
                if a == 0:
                    pe.wait_ge(proj_kept, blocks_needed)
                    pe.wait_ge(keys_ready, 2 * g + 2)
                    if g:
                        pe.wait_ge(states_ready, g)
                else:
                    pe.wait_ge(level_kept, 8 * g + a)
                for h in range(2):
                    for c in range(4):
                        chunk = slice(c * P, (c + 1) * P)
                        if a == 0:
                            out_, rhs = bank[2 + h][:, chunk], qp[:, g % 2, h, chunk]
                        else:
                            m = LEVELS[a - 1]
                            out_ = bank[2 + a % 2][:, (4 * h + c) * 64:(4 * h + c + 1) * 64]
                            rhs = qp[:, g % 2, h, chunk].rearrange("p (b two e) -> p b two e", two=2, e=m)[:, :, 1, :]
                        mm = pe.matmul(out_, ks[:, g % 2, h, chunk], rhs, start=True, stop=True)
                mm.then_inc(level_done, 1)

            def turn_keys(g, K0):
                pe.wait_ge(level_kept, 8 * g + 8)
                pe.wait_ge(h_lo_done, 2 * (K0 + g)) if K0 + g else None
                for h in range(2):
                    for c in range(4):
                        mm = pe.transpose(bank[4 + h][:, c * P:(c + 1) * P], ks[:, g % 2, h, c * P:(c + 1) * P], ident[:])
                    mm.then_inc(keys_turned, 1)

            def updates(g, blocks_needed):
                pe.wait_ge(keys_tok_ready, 2 * g + 2)
                pe.wait_ge(proj_kept, blocks_needed)
                for h in range(2):
                    for c in range(3):
                        mm = pe.matmul(bank[2 + h][:, c * P:(c + 1) * P], keys_tok[:, h, c * P:(c + 1) * P],
                                       values[:, g % 2, c, h * P:(h + 1) * P], start=True, stop=True)
                mm.then_inc(updates_done, 1)

            def outputs(g):
                pe.wait_ge(states_ready, g + 1)
                for c in range(4):
                    for h in range(2):
                        out_ = bank[4 + c // 2][:, (c % 2) * GW + h * P:(c % 2) * GW + (h + 1) * P]
                        chunk = slice(c * P, (c + 1) * P)
                        mm = pe.matmul(out_, within[:, h, chunk], values[:, g % 2, c, h * P:(h + 1) * P],
                                       start=True, stop=c == 0)
                        if c:
                            mm = pe.matmul(out_, qp[:, g % 2, h, chunk], state[:, h, c - 1, :], start=False, stop=True)
                    if c % 2:
                        mm.then_inc(outputs_done, 1)

            def turn_out(src):
                for j in range(2):
                    for t in range(NT):
                        mm = pe.transpose(bank[4 + j][:, t * P:(t + 1) * P], src[:, t, j * P:(j + 1) * P], ident[:])
                    mm.then_inc(out_turned, 1)

            pe.wait_ge(consts_ready, 2)
            pe.wait_ge(small_loaded, 48)
            pe.transpose(bank[3][:, 0:16], lb_rows[:], ident[0:16, 0:16]).then_inc(lb_turned, 1)
            for n, (kind, wi, ln, _w) in enumerate(phases):
                s0, K0 = bases[n]
                if kind == "ffn":
                    G0 = NG * ffn_index[n]
                    begin(n, ffn_first_two(s0))
                    with pe.Fori(0, NG - 1) as i:
                        up(s0 + 2, G0 + 1, up1_done, gate_done, 0, i)
                        down(s0 + 3, K0, bank[4:8], i)
                        up(s0 + 4, G0 + 1, up3_done, hid_done, 2, i)
                    down(s0 + 3 * NG - 1, K0 + NG - 1, LAST_BANKS)
                else:
                    slabs, plan = mixer_slabs(kind), mixer_schedule(kind)
                    banks = bank[0:2] if kind == "attn" else bank[6:8]
                    first = block_base[n]
                    block = first + 4
                    begin(n, mixer_first_two(s0, slabs))
                    for step in plan:
                        what, g = step[0], step[1]
                        if what == "quarter":
                            name, group = slabs[step[1]]
                            if name == "down":
                                if step[2] == 0 and kind == "attn":
                                    pe.wait_ge(proj_kept, block)
                                down_quarter(s0 + step[1], K0 + group, step[2], banks)
                            else:
                                if kind == "attn" and step[2] == 0:
                                    downs = sum(x[0] == "down" for x in slabs[:step[1]])
                                    pe.wait_ge(y_added, 8 * (K0 + downs) + FREE_AT_START)
                                projected(s0 + step[1], name, step[2], block)
                                block += step[2] % 2
                        elif what == "scores":
                            group = attention_unit(step[1])[0] // 4
                            scores(step[1], first + blocks_until(kind, "q", group))
                        elif what == "turn_probs":
                            turn_probs(step[1], K0 + attention_unit(step[1])[0] // 4)
                        elif what == "values":
                            group = attention_unit(step[1])[0] // 4
                            weigh_values(step[1], first + (blocks_until(kind, "vb", group) if group > 1 else 2))
                        elif what == "level":
                            level_products(g, step[2], first + blocks_until(kind, "q", g))
                        elif what == "turn_keys":
                            turn_keys(g, K0)
                        elif what == "updates":
                            updates(g, first + blocks_until(kind, "v", g))
                        elif what == "outputs":
                            outputs(g)
                        elif kind == "attn":
                            pe.wait_ge(head_kept, 4 * g + 4)
                            pe.wait_ge(probs_t_act, UNITS[g + 1])
                            pe.wait_ge(probs_t_dve, two_bank_units(UNITS[g + 1]))
                            turn_out(att_out)
                        else:
                            pe.wait_ge(normed_ready, g + 1)
                            turn_out(normed)
                    for t in range(NT):
                        down_quarter(s0 + len(slabs) - 1, K0 + 3, t, LAST_BANKS)


_INS = ["x", "ffn_w1", "ffn_w3", "ffn_w2", "ln_g", "ln_b", "attn_w_in", "attn_sinks", "attn_w_out",
        "hgrn_w_in", "hgrn_norm_g", "hgrn_w_out", "hgrn_lower_bounds"]


def kernel(**inputs):
    import concourse.bacc as bacc
    from concourse.bass_utils import run_bass_kernel_spmd

    nc = bacc.Bacc("TRN2", target_bir_lowering=False, num_devices=1)
    arrays, args = {}, []
    for name in _INS:
        a = np.ascontiguousarray(inputs[name])
        arrays[f"in_{name}"] = a
        args.append(nc.dram_tensor(f"in_{name}", a.shape, mybir.dt.from_np(a.dtype), kind="ExternalInput").ap())
    args.append(nc.dram_tensor("out_x", (1, T, D), F32, kind="ExternalOutput").ap())
    build_trunk(nc, *args)
    return run_bass_kernel_spmd(nc, [arrays], core_ids=[0]).results[0]["out_x"]
```

```python
import numpy as np
import concourse.bass as bass
from concourse import mybir
from contextlib import ExitStack

F32 = mybir.dt.float32
F32R = mybir.dt.float32r
ALU = mybir.AluOpType
ACT = mybir.ActivationFunctionType
AX = mybir.AxisListType

P = 128
D = 1024
T = 512
DFF = 2816
NT = T // P
DC = D // P
GW = 256
NG = DFF // GW
SLAB = 2048
RING = 3
HALF = D // 2
ALPHA = 4.0 ** 0.25
LN_EPS = 1e-5 / (ALPHA * ALPHA)
RMS_EPS = 1e-6
LEVELS = [1, 2, 4, 8, 16, 32, 64]
MASK_STEPS = 1 + 2 * len(LEVELS)
TABLE_STEPS = 4 * 3 + 4 * 2
ARENA = 15360
FREE_AT_START = 4
HD = 64
SCALE = HD ** -0.5
SLOPES = [2.0 ** (-8.0 * (i + 1) / 16) for i in range(16)]
WINDOW = 128
FAR = 1.0e30

PHASES = [("ffn", (0, 0), (0, 0), 0.5), ("attn", 0, (0, 1), 1.0), ("ffn", (0, 1), (0, 2), 0.5),
          ("ffn", (1, 0), (1, 0), 0.5), ("hgrn", 0, (1, 1), 1.0), ("ffn", (1, 1), (1, 2), 0.5)]
SIZES = {"ffn": (3 * NG, NG - 1, NG), "attn": (13, 4, 4), "hgrn": (20, 4, 4)}


def layout(phases):
    out, s, k, h = [], 0, 0, 0
    for ph in phases:
        out.append((s, k, h))
        sizes = SIZES[ph[0]]
        s, k, h = s + sizes[0], k + sizes[1], h + sizes[2]
    return out, s


HGRN_PART = {"q": 0, "f": 1, "v": 2, "g": 3}
MIXER_SLABS = {
    "attn": ([("kv", 0), ("q", 0)],
             [[("q", 1), ("kb", 2), ("q", 2), ("vb", 2), ("down", 0), ("kb", 3), ("q", 3), ("vb", 3), ("down", 1),
               ("down", 2)]]),
    "hgrn": ([("f", 0), ("q", 0)],
             [[("v", 0), ("g", 0), ("f", 1), ("q", 1), ("g", 1)], [("v", 1), ("down", 0), ("f", 2), ("q", 2), ("g", 2)],
              [("v", 2), ("f", 3), ("q", 3), ("down", 1)], [("v", 3), ("g", 3), ("down", 2)]]),
}
UNITS = [0, 4, 8, 16, 24]
TURN_OUT_AT = {5: 0, 12: 1, 19: 2}
WITHOUT_FILL = (17, 20, 22)


def mixer_slabs(kind):
    first, between = MIXER_SLABS[kind]
    return first + [x for names in between for x in names] + [("down", 3)]


def mixer_blocks(kind):
    return 2 * sum(name != "down" for name, _ in mixer_slabs(kind))


def blocks_until(kind, name, group):
    slabs = mixer_slabs(kind)
    return 2 * sum(x[0] != "down" for x in slabs[:slabs.index((name, group)) + 1])


def mixer_schedule(kind):
    quarters = iter([("quarter", s, c) for s in range(2, len(mixer_slabs(kind)) - 1) for c in range(4)])

    def fill(n):
        return [next(quarters) for _ in range(n)]

    steps = []
    if kind == "attn":
        steps += [("scores", 0)] + fill(1) + [("scores", 1)] + fill(1)
        for u in range(UNITS[4]):
            steps.append(("turn_probs", u))
            if u + 2 < UNITS[4]:
                steps.append(("scores", u + 2))
            steps += fill(u not in WITHOUT_FILL)
            if u in TURN_OUT_AT:
                steps.append(("turn_out", TURN_OUT_AT[u]))
            steps += [("values", u)] + fill(2 <= u <= UNITS[3])
        return steps + [("turn_out", 3)] + fill(2)
    for g in range(4):
        own = [("level", g, a) for a in range(0 if g == 0 else 2, 8)] + [("turn_keys", g), ("updates", g)]
        n = 4 * len(MIXER_SLABS[kind][1][g]) - 4
        for at, step in enumerate(own):
            steps += [step] + fill(n * (at + 1) // len(own) - n * at // len(own))
        steps.append(("outputs", g))
        if g < 3:
            steps.append(("level", g + 1, 0))
        steps += fill(1) + [("norm", g)] + fill(1)
        if g < 3:
            steps.append(("level", g + 1, 1))
        steps += fill(2) + [("turn_out", g)] if g < 3 else [("turn_out", g)] + fill(2)
    return steps


def splits(plan, urgent, reach):
    out = {}
    for at, step in enumerate(plan):
        if step[0] == "quarter" and step[2] == 3:
            near = [i for i in range(at + 1, min(at + 1 + reach, len(plan))) if plan[i][0] in urgent]
            out.setdefault(near[0] if near else at, []).append(step[1] + RING)
    return out


SWA_UNIT = ([(0, [0]), (1, [0, 1]), (2, [1, 2]), (3, [2, 3])], P)
MOBA_UNITS = [([(0, [0]), (2, [0, 1, 2]), (1, [0, 1])], 0), ([(3, [0, 1, 2, 3])], 0)]


def attention_unit(u):
    if u < 8:
        return u, SWA_UNIT[0], SWA_UNIT[1], True
    return 8 + (u - 8) // 2, *MOBA_UNITS[u % 2], u % 2 == 1


def decay_at(m):
    return 2 * T - 4 * T // m


def two_bank_units(u):
    return min(u, 8) + (max(u - 8, 0) + 1) // 2


def build_trunk(nc, x_in, w1, w3, w2, ln_g, ln_b, aw_in, sinks, aw_out, hw_in, hnorm, hw_out, lbs_in, out,
                phases=None):
    phases = PHASES if phases is None else phases
    bases, n_slabs = layout(phases)
    ffn_index = [sum(p[0] == "ffn" for p in phases[:n]) for n in range(len(phases))]
    last_phase = len(phases) - 1
    before = [[p[0] for p in phases[:n] if p[0] != "ffn"] for n in range(len(phases))]
    block_base = [sum(mixer_blocks(kind) for kind in kinds) for kinds in before]
    out_base = [8 * len(kinds) for kinds in before]

    with ExitStack() as ctx:
        def sb(name, shape, dt=F32):
            return ctx.enter_context(nc.sbuf_tensor(name, shape, dt))

        def sem(name):
            return ctx.enter_context(nc.semaphore(name))

        raw = sb("raw", [P, RING, SLAB])
        w_hi = sb("w_hi", [P, RING, SLAB], F32R)
        w_lo = sb("w_lo", [P, RING, SLAB], F32R)
        x = sb("x", [P, NT, D])
        xt_hi = sb("xt_hi", [P, DC, T], F32R)
        xt_lo = sb("xt_lo", [P, DC, T], F32R)
        lng = sb("lng", [P, D])
        lnb = sb("lnb", [P, D])
        stats = sb("stats", [P, 2, 6])
        meanvar = sb("meanvar", [P, NT, 2])
        vareps = sb("vareps", [P, NT])
        rstd = sb("rstd", [P, NT])
        neghalf = sb("neghalf", [P, 8])
        ident = sb("ident", [P, P])
        gate = sb("gate", [P, 2, T])
        hid = sb("hid", [P, 2, T])
        h_hi = sb("h_hi", [P, 2, T], F32R)
        h_lo = sb("h_lo", [P, 2, T], F32R)
        psum = ctx.enter_context(nc.psum_tensor("psum", [P, 8 * T], F32))
        bank = [psum[:, i * T:(i + 1) * T] for i in range(8)]

        arena = sb("arena", [P, ARENA])
        cursor = [0]

        def cut(*shape):
            n = int(np.prod(shape))
            part = arena[:, cursor[0]:cursor[0] + n]
            cursor[0] += n
            assert cursor[0] <= ARENA
            if len(shape) == 2:
                return part.rearrange("p (a b) -> p a b", b=shape[1])
            if len(shape) == 3:
                return part.rearrange("p (a b c) -> p a b c", b=shape[1], c=shape[2])
            return part

        q_t = cut(2, 2, T)
        k_swa = cut(2, T)
        k_moba = cut(2, 2, T)
        v_swa = cut(NT, P)
        v_moba = cut(2, NT, GW)
        dist_swa = cut(7 * P)
        dist_moba = [cut(6 * P), cut(4 * P)]
        probs = cut(3, 7 * P)
        probs_t = cut(2, 7 * P)
        att_out = [cut(NT, GW), gate[:].rearrange("p j t -> p (j t)").rearrange("p (t n) -> p t n", n=GW)]
        cursor[0] = 0
        decay = cut(2, 2, T)
        qp = cut(2, 2, T)
        ks = cut(2, 2, T)
        values = cut(2, NT, GW)
        out_gate = cut(2, NT, GW)
        block_decay = cut(2 * T)
        squares = block_decay[:, 0:2 * T].rearrange("p (a b) -> p a b", b=P)
        within = cut(2, T)
        keys_tok = cut(2, T)
        normed = keys_tok.rearrange("p h n -> p (h n)").rearrange("p (t n) -> p t n", n=GW)
        state = cut(2, 3, P)
        sig_pos, sig_neg = gate, hid

        def last_h(part, j):
            return part[:, 2 * j:2 * j + 2, T // 2:T]

        neg_max = sb("neg_max", [P, 3, 4])
        sums = sb("sums", [P, 4, 4])
        sink_part = sb("sink_part", [P, 4, 4])
        inv_sum = sb("inv_sum", [P, 4])
        total = sb("total", [P, 4])
        sink_b = sb("sink_b", [P, 8])
        neg_sink = sb("neg_sink", [P, 8])
        norm_b = sb("norm_b", [P, P])
        lb_rows = sb("lb_rows", [16, P])
        lb_t = sb("lb_t", [P, 2, 8])
        lb_m = sb("lb_m", [P, 8])
        lb_e = sb("lb_e", [P, 2, 8])
        lb_r = sb("lb_r", [P, 8])
        lower = sb("lower", [P, 8])
        span = sb("span", [P, 8])
        pair_mask_f = hid[:, 0, 0:7 * 64].rearrange("p (a b) -> p a b", b=64)
        pair_mask = sb("pair_mask", [P, 7, 64], mybir.dt.uint8)
        mean_sq = sb("mean_sq", [P, 8])
        rms_in = sb("rms_in", [P, 8])
        rms = sb("rms", [P, 8])

        x_loaded = [sem(f"x_loaded{t}") for t in range(NT)]
        ident_zeroed = sem("ident_zeroed")
        consts_ready = sem("consts_ready")
        raw_landed = [sem(f"raw_landed{i}") for i in range(RING)]
        hi_ready = sem("hi_ready")
        lo_ready = sem("lo_ready")
        up1_done = sem("up1_done")
        up3_done = sem("up3_done")
        gate_done = sem("gate_done")
        hid_done = sem("hid_done")
        h_hi_done = sem("h_hi_done")
        h_lo_done = sem("h_lo_done")
        y_done = sem("y_done")
        first_down_of_two = sem("first_down_of_two")
        y_added = sem("y_added")
        par_loaded = [sem(f"par_loaded{i}") for i in range(2)]
        stat_done = sem("stat_done")
        var_ready = sem("var_ready")
        rstd_ready = sem("rstd_ready")
        centred = sem("centred")
        ln_done = sem("ln_done")
        turn_done = sem("turn_done")
        xt_hi_done = sem("xt_hi_done")
        xt_lo_done = sem("xt_lo_done")
        out_stored = sem("out_stored")
        small_loaded = sem("small_loaded")
        lb_turned = sem("lb_turned")
        lb_exp = sem("lb_exp")
        set_up = sem("set_up")
        masks_step = sem("masks_step")
        proj_done = sem("proj_done")
        proj_kept = sem("proj_kept")
        kv_halves = sem("kv_halves")
        kv_copied = [sem(f"kv_copied{i}") for i in range(2)]
        scores_done = sem("scores_done")
        scores_kept = sem("scores_kept")
        max_ready = sem("max_ready")
        neg_max_ready = sem("neg_max_ready")
        exp_done = sem("exp_done")
        probs_turned = sem("probs_turned")
        probs_t_act = sem("probs_t_act")
        probs_t_dve = sem("probs_t_dve")
        head_done = sem("head_done")
        head_kept = sem("head_kept")
        out_turned = sem("out_turned")
        keys_ready = sem("keys_ready")
        level_done = sem("level_done")
        level_kept = sem("level_kept")
        level_step = sem("level_step")
        gate_normed = sem("gate_normed")
        keys_turned = sem("keys_turned")
        keys_tok_ready = sem("keys_tok_ready")
        updates_done = sem("updates_done")
        states_ready = sem("states_ready")
        outputs_done = sem("outputs_done")
        squares_done = sem("squares_done")
        rms_asked = sem("rms_asked")
        rms_ready = sem("rms_ready")
        normed_ready = sem("normed_ready")

        users = []
        for n, ph in enumerate(phases):
            K0 = bases[n][1]
            if ph[0] == "ffn":
                G0 = NG * ffn_index[n]
                users += [(up1_done, 2 * G0 + 2, 2), (up3_done, 2 * G0 + 2, 2)]
                for g in range(1, NG - 1):
                    users += [(up1_done, 2 * (G0 + g) + 2, 2), (y_done, 8 * (K0 + g), 8),
                              (up3_done, 2 * (G0 + g) + 2, 2)]
                users += [(up1_done, 2 * (G0 + NG), 2), (up3_done, 2 * (G0 + NG), 2),
                          (first_down_of_two, ffn_index[n] + 1, 1), (y_done, 8 * (K0 + NG - 1), 8)]
            else:
                blocks = block_base[n]
                for name, g in mixer_slabs(ph[0]):
                    if name == "down":
                        users.append((y_done, 8 * (K0 + g + 1), 8))
                    else:
                        blocks += 2
                        users.append((proj_done, blocks, 2))

        LAST_BANKS = bank[4:8] + bank[0:4]

        def proj_bank(s, j):
            return 2 * s + j if s < 2 else j

        block = ctx.enter_context(nc.Block())

        def upto(at, i, by=1):
            return at if i is None else at + by * i

        @block.sync
        def _(sp):
            def load_slab(s, src, i=None):
                if s >= RING or i is not None:
                    sp.wait_ge(lo_ready, upto(s - RING + 1, i, RING))
                dst = raw[:, s % RING, :]
                sp.dma_start(dst.rearrange("p (c n) -> p c n", n=src.shape[-1]), src).then_inc(raw_landed[s % RING], 16)

            def load_params(n):
                l, k = phases[n][2]
                if n:
                    sp.wait_ge(ln_done, NT * n)
                sp.dma_start(lng[:], ln_g[l, k:k + 1, :].broadcast_to([P, D])).then_inc(par_loaded[0], 16)
                sp.dma_start(lnb[:], ln_b[l, k:k + 1, :].broadcast_to([P, D])).then_inc(par_loaded[1], 16)

            def up_slab(w, g):
                return w[:, bass.ds(g * GW, GW)].rearrange("(c p) n -> p c n", p=P)

            def down_slab(w, g):
                return w[bass.ds(g * GW, GW), :].rearrange("(c p) n -> p c n", p=P)

            def load_x(t):
                sp.dma_start(x[:, t, :], x_in[0, t * P:(t + 1) * P, :]).then_inc(x_loaded[t], 16)

            def load_small():
                sp.dma_start(sink_b[:], sinks[0:1, :].broadcast_to([P, 8])).then_inc(small_loaded, 16)
                sp.dma_start(norm_b[:], hnorm[0:1, :].broadcast_to([P, P])).then_inc(small_loaded, 16)
                sp.dma_start(lb_rows[:], lbs_in.rearrange("l (h k) -> (l h) k", k=P)).then_inc(small_loaded, 16)

            load_x(0)
            for n, (kind, wi, _, _) in enumerate(phases):
                s0 = bases[n][0]
                if kind == "ffn":
                    l, f = wi
                    a, b, c = w1[l, f], w3[l, f], w2[l, f]
                    load_slab(s0, up_slab(a, 0))
                    if n == 0:
                        load_x(1)
                    load_slab(s0 + 1, up_slab(b, 0))
                    if n == 0:
                        load_x(2)
                        load_x(3)
                        load_small()
                    load_slab(s0 + 2, up_slab(a, 1))
                    load_params(n)
                    load_slab(s0 + 3, down_slab(c, 0))
                    load_slab(s0 + 4, up_slab(b, 1))
                    with sp.Fori(1, NG - 2) as i:
                        load_slab(s0 + 2, up_slab(a, i + 1), i)
                        load_slab(s0 + 3, down_slab(c, i), i)
                        load_slab(s0 + 4, up_slab(b, i + 1), i)
                    for s, src in enumerate((up_slab(a, NG - 1), up_slab(b, NG - 1),
                                             down_slab(c, NG - 2), down_slab(c, NG - 1))):
                        load_slab(s0 + 3 * NG - 4 + s, src)
                else:
                    for s, (name, g) in enumerate(mixer_slabs(kind)):
                        if s == RING:
                            load_params(n)
                        if kind == "attn":
                            swa, moba = 8 * HD, 8 * HD + 4 * HD
                            col = {"q": g * GW if g < 2 else moba + (g - 2) * GW, "kv": swa,
                                   "kb": moba + 512 + (g - 2) * GW, "vb": moba + 1024 + (g - 2) * GW}
                            src = down_slab(aw_out[0], g) if name == "down" else \
                                aw_in[0][:, col[name]:col[name] + GW].rearrange("(c p) n -> p c n", p=P)
                        else:
                            src = down_slab(hw_out[0], g) if name == "down" else \
                                hw_in[0][:, HGRN_PART[name] * D + g * GW:HGRN_PART[name] * D + (g + 1) * GW]\
                                .rearrange("(c p) n -> p c n", p=P)
                        load_slab(s0 + s, src)
                        if n == 0 and s == 0:
                            load_x(1)
                        if n == 0 and s == 1:
                            load_x(2)
                            load_x(3)
                            load_small()
            for t in range(NT):
                sp.wait_ge(ln_done, NT * last_phase + t + 1)
                sp.dma_start(out[0, t * P:(t + 1) * P, :], x[:, t, :]).then_inc(out_stored, 16)
            sp.wait_ge(out_stored, 16 * NT)

        @block.gpsimd
        def _(pool):
            pool.memset(neghalf[:], -0.5).then_inc(consts_ready, 1)
            pool.memset(ident[:], 0.0).then_inc(ident_zeroed, 1)
            pool.wait_ge(ident_zeroed, 1)
            pool.affine_select(out=ident[:], in_=ident[:], compare_op=ALU.not_equal, fill=1.0, base=0,
                               pattern=[[-1, P]], channel_multiplier=1).then_inc(consts_ready, 1)

            steps = [0]

            def then(op):
                op.then_inc(masks_step, 1)
                steps[0] += 1
                pool.wait_ge(masks_step, steps[0])

            def distances(table, tile, keys, window):
                n = len(keys) * P
                then(pool.iota(table, pattern=[[-1, n]], base=(tile - keys[0]) * P, channel_multiplier=1,
                               allow_small_or_imprecise_dtypes=True))
                then(pool.affine_select(out=table, in_=table, compare_op=ALU.is_ge, fill=FAR,
                                        base=(tile - keys[0]) * P, pattern=[[-1, n]], channel_multiplier=1))
                if window:
                    then(pool.affine_select(out=table, in_=table, compare_op=ALU.is_ge, fill=FAR,
                                            base=WINDOW - 1 - (tile - keys[0]) * P, pattern=[[1, n]],
                                            channel_multiplier=-1))

            def attention_tables():
                for table, (tiles, _) in [(dist_swa, SWA_UNIT), (dist_moba[0], MOBA_UNITS[0]), (dist_moba[1], MOBA_UNITS[1])]:
                    at = 0
                    for tile, keys in tiles:
                        distances(table[:, at:at + len(keys) * P], tile, keys, table is dist_swa)
                        at += len(keys) * P

            then(pool.memset(pair_mask_f, 1.0))
            for a, m in enumerate(LEVELS):
                view = pair_mask_f[:, a, :].rearrange("p (b e) -> p b e", e=m)
                then(pool.affine_select(out=view, in_=view, compare_op=ALU.is_ge, fill=0.0, base=0,
                                        pattern=[[-2 * m, 64 // m], [0, m]], channel_multiplier=1))
                then(pool.affine_select(out=view, in_=view, compare_op=ALU.is_ge, fill=0.0, base=m - 1,
                                        pattern=[[2 * m, 64 // m], [0, m]], channel_multiplier=-1))

            def low(s, i=None):
                pool.wait_ge(hi_ready, upto(s + 1, i, RING))
                pool.tensor_tensor(w_lo[:, s % RING, :], raw[:, s % RING, :], w_hi[:, s % RING, :].bitcast(F32),
                                   ALU.subtract).then_inc(lo_ready, 1)

            def norm_powers(n, tiles):
                for t in tiles:
                    pool.wait_ge(var_ready, NT * n + t + 1)
                    pool.tensor_tensor(rstd[:, t:t + 1], vareps[:, t:t + 1], neghalf[:, 0:1],
                                       ALU.pow).then_inc(rstd_ready, 1)

            pool.wait_ge(lo_ready, 2)
            low(2)
            for n, (kind, _, _, _) in enumerate(phases):
                s0 = bases[n][0]
                if kind == "ffn":
                    with pool.Fori(0, NG - 1) as i:
                        for j in range(RING):
                            low(s0 + RING + j, i)
                    for j, tiles in enumerate(((0, 1), (2, 3), ())):
                        if n < last_phase:
                            low(s0 + 3 * NG + j)
                        norm_powers(n, tiles)
                else:
                    slabs, plan = mixer_slabs(kind), mixer_schedule(kind)
                    if kind == "attn":
                        attention_tables()
                    low(s0 + RING)
                    low(s0 + RING + 1)
                    split_at = splits(plan, ("outputs",), 2)
                    for at, step in enumerate(plan):
                        if step[0] == "quarter" and step[2] == 3 and slabs[step[1]][0] == "g":
                            g = slabs[step[1]][1]
                            pool.wait_ge(small_loaded, 48)
                            pool.wait_ge(proj_kept, block_base[n] + blocks_until(kind, "g", g))
                            view = out_gate[:, g % 2].rearrange("p t (h n) -> p (t h) n", n=P)
                            pool.tensor_tensor(view, view, norm_b[:, None, :].broadcast_to([P, 8, P]),
                                               ALU.mult).then_inc(gate_normed, 1)
                        if step[0] == "outputs":
                            pool.wait_ge(rms_asked, step[1] + 1)
                            pool.tensor_tensor(rms[:], rms_in[:], neghalf[:], ALU.pow).then_inc(rms_ready, 1)
                        for s in split_at.get(at, ()):
                            if s <= len(slabs) and s0 + s < n_slabs:
                                low(s0 + s)
                    for j, tiles in ((0, (0, 1)), (1, (2, 3)), (2, ())):
                        if j and n < last_phase:
                            low(s0 + len(slabs) + j)
                        norm_powers(n, tiles)

        @block.scalar
        def _(act):
            def high(s, i=None):
                act.wait_ge(raw_landed[s % RING], upto(16 * (s // RING + 1), i, 16))
                if s >= RING:
                    used, count, by = users[s - RING]
                    act.wait_ge(used, upto(count, i, by))
                act.activation(w_hi[:, s % RING, :], raw[:, s % RING, :], ACT.Copy).then_inc(hi_ready, 1)

            def turn_high(turn, t):
                for b in range(2):
                    act.wait_ge(turn_done, 8 * turn + 2 * t + b + 1)
                    act.activation(xt_hi[:, 4 * b:4 * b + 4, t * P:(t + 1) * P],
                                   bank[4 + 2 * (t % 2) + b].rearrange("p (c n) -> p c n", n=P),
                                   ACT.Copy).then_inc(xt_hi_done, 1)

            def gates(G, i=None):
                for j in range(2):
                    act.wait_ge(up1_done, upto(2 * G + j + 1, i, 2))
                    if G:
                        act.wait_ge(hid_done, upto(2 * (G - 1) + j + 1, i, 2))
                    act.activation(gate[:, j, :], bank[j][:], ACT.Silu).then_inc(gate_done, 1)

            def hid_high(G, K, i=None):
                for j in range(2):
                    act.wait_ge(hid_done, upto(2 * G + j + 1, i, 2))
                    if K:
                        act.wait_ge(y_done, upto(8 * K, i, 8))
                    act.activation(h_hi[:, j, :], hid[:, j, :], ACT.Copy).then_inc(h_hi_done, 1)

            def turn_all_high(turn, spare_slab):
                turn_high(turn, 0)
                turn_high(turn, 1)
                high(spare_slab)
                turn_high(turn, 2)
                turn_high(turn, 3)

            turn_high(0, 0)
            high(0)
            turn_high(0, 1)
            high(1)
            turn_high(0, 2)
            turn_high(0, 3)
            high(2)
            act.wait_ge(lb_turned, 1)
            act.activation(lb_t[:].rearrange("p l h -> p (l h)"), bank[4][:, 0:16], ACT.Copy).then_inc(lb_exp, 1)
            act.wait_ge(set_up, 2)
            act.activation(lb_e[:], lb_t[:], ACT.Exp).then_inc(lb_exp, 1)

            def keep_block(kind, slabs, s, j, block):
                name, g = slabs[s]
                src = bank[proj_bank(s, j)]
                two_tiles = src.rearrange("p (t n) -> p t n", n=GW)
                act.wait_ge(proj_done, block + 1)
                if name == "q" and kind == "attn":
                    op = act.activation(q_t[:, g % 2, j, :], src, ACT.Copy, scale=SCALE)
                elif name == "kv" and j == 0:
                    act.activation(k_swa[0:HD, 0, :], src[0:HD, :], ACT.Copy).then_inc(kv_halves, 1)
                    op = act.activation(k_swa[HD:P, 1, :], src[HD:P, :], ACT.Copy)
                elif name == "kv":
                    op = act.activation(v_swa, src.rearrange("p (t n) -> p t n", n=P), ACT.Copy)
                elif name == "kb":
                    op = act.activation(k_moba[:, g % 2, j, :], src, ACT.Copy)
                elif name == "vb":
                    op = act.activation(v_moba[:, g % 2, 2 * j:2 * j + 2, :], two_tiles, ACT.Copy)
                elif name == "f":
                    if g:
                        act.wait_ge(keys_ready, 2 * (g - 1) + j + 1)
                    act.activation(sig_pos[:, j, :], src, ACT.Sigmoid)
                    op = act.activation(sig_neg[:, j, :], src, ACT.Sigmoid, scale=-1.0)
                elif name == "q":
                    op = act.activation(qp[:, g % 2, j, :], src, ACT.Silu)
                elif name == "g":
                    op = act.activation(out_gate[:, g % 2, 2 * j:2 * j + 2, :], two_tiles, ACT.Silu)
                else:
                    op = act.activation(values[:, g % 2, 2 * j:2 * j + 2, :], two_tiles, ACT.Copy)
                op.then_inc(proj_kept, 1)
                if name == "kv" and j == 0:
                    act.wait_ge(kv_halves, 1)
                    act.dma_start(k_swa[HD:P, 0, :], k_swa[0:HD, 0, :]).then_inc(kv_copied[0], 16)
                    act.wait_ge(proj_kept, block + 1)
                    act.dma_start(k_swa[0:HD, 1, :], k_swa[HD:P, 1, :]).then_inc(kv_copied[1], 16)

            def exponentials(u):
                head, tiles, _, _ = attention_unit(u)
                act.wait_ge(neg_max_ready, u + 1)
                at = 0
                for n_, (tile, keys) in enumerate(tiles):
                    part = probs[:, u % 3, at:at + len(keys) * P]
                    op = act.activation(part, part, ACT.Exp, bias=neg_max[:, u % 3, n_:n_ + 1],
                                        accum_out=sums[:, head % 4, tile:tile + 1])
                    at += len(keys) * P
                if head < 8:
                    op = act.activation(sink_part[:, head % 4, :], neg_max[:, u % 3, :], ACT.Exp,
                                        bias=sink_b[:, head:head + 1])
                op.then_inc(exp_done, 1)

            def probs_first_bank(u):
                act.wait_ge(probs_turned, u + 1)
                act.activation(probs_t[:, u % 2, 0:4 * P], bank[4], ACT.Copy).then_inc(probs_t_act, 1)

            def turned_out_high(outs, K, last):
                for j in range(2):
                    act.wait_ge(out_turned, outs + j + 1)
                    src, dst = bank[4 + j], h_hi[:, j, :]
                    if last:
                        src, dst = src.rearrange("p (c n) -> p c n", c=2), last_h(xt_hi, j)
                    elif K:
                        act.wait_ge(y_done, 8 * K)
                    act.activation(dst, src, ACT.Copy).then_inc(h_hi_done, 1)

            for n, (kind, _, _, _) in enumerate(phases):
                s0, K0, H0 = bases[n]
                if kind == "ffn":
                    G0 = NG * ffn_index[n]
                    gates(G0)
                    high(s0 + 3)
                    hid_high(G0, K0)
                    high(s0 + 4)
                    with act.Fori(0, NG - 2) as i:
                        gates(G0 + 1, i)
                        high(s0 + 5, i)
                        high(s0 + 6, i)
                        hid_high(G0 + 1, K0 + 1, i)
                        high(s0 + 7, i)
                    gates(G0 + NG - 1)
                    high(s0 + 3 * NG - 1)
                    for j in range(2):
                        act.wait_ge(hid_done, 2 * (G0 + NG))
                        act.activation(last_h(xt_hi, j), hid[:, j, :].rearrange("p (c n) -> p c n", c=2),
                                       ACT.Copy).then_inc(h_hi_done, 1)
                    if n < last_phase:
                        high(s0 + 3 * NG)
                        high(s0 + 3 * NG + 1)
                else:
                    slabs, plan = mixer_slabs(kind), mixer_schedule(kind)
                    block, outs = block_base[n], out_base[n]
                    for s in range(2):
                        for j in range(2):
                            keep_block(kind, slabs, s, j, block)
                            block += 1
                        high(s0 + s + RING)
                    split_at = splits(plan, ("turn_out", "outputs"), 1)
                    for at, step in enumerate(plan):
                        if step[0] == "quarter":
                            name = slabs[step[1]][0]
                            if name != "down" and step[2] % 2 == 1:
                                keep_block(kind, slabs, step[1], step[2] // 2, block)
                                block += 1
                        elif step[0] == "scores":
                            exponentials(step[1])
                        elif step[0] == "turn_probs":
                            probs_first_bank(step[1])
                        elif step[0] == "turn_keys":
                            for h in range(2):
                                act.wait_ge(keys_turned, 2 * step[1] + h + 1)
                                act.activation(keys_tok[:, h, :], bank[4 + h], ACT.Copy).then_inc(keys_tok_ready, 1)
                        elif step[0] == "outputs":
                            for b in range(2):
                                act.wait_ge(outputs_done, 2 * step[1] + b + 1)
                                act.activation(squares[:, 4 * b:4 * b + 4, :],
                                               bank[4 + b].rearrange("p (a n) -> p a n", n=P),
                                               ACT.Square).then_inc(squares_done, 1)
                        elif step[0] == "turn_out":
                            turned_out_high(outs + 2 * step[1], K0 + step[1], step[1] == 3)
                        for s in split_at.get(at, ()):
                            if s0 + s < n_slabs:
                                high(s0 + s)
                if n < last_phase:
                    turn_all_high(n + 1, bases[n + 1][0] + 2)

        @block.vector
        def _(dve):
            def turn_low(turn, t):
                for b in range(2):
                    dve.wait_ge(xt_hi_done, 8 * turn + 2 * t + b + 1)
                    part = (slice(None), slice(4 * b, 4 * b + 4), slice(t * P, (t + 1) * P))
                    dve.tensor_tensor(xt_lo[part], bank[4 + 2 * (t % 2) + b].rearrange("p (c n) -> p c n", n=P),
                                      xt_hi[part].bitcast(F32), ALU.subtract).then_inc(xt_lo_done, 1)

            def hiddens(G, i=None):
                for j in range(2):
                    dve.wait_ge(gate_done, upto(2 * G + j + 1, i, 2))
                    dve.wait_ge(up3_done, upto(2 * G + j + 1, i, 2))
                    dve.tensor_tensor(hid[:, j, :], bank[2 + j][:], gate[:, j, :], ALU.mult).then_inc(hid_done, 1)

            def hid_low(H, i=None):
                for j in range(2):
                    dve.wait_ge(h_hi_done, upto(2 * H + j + 1, i, 2))
                    dve.tensor_tensor(h_lo[:, j, :], hid[:, j, :], h_hi[:, j, :].bitcast(F32),
                                      ALU.subtract).then_inc(h_lo_done, 1)

            def add_piece(K, k, weight, banks, i=None):
                t, half = divmod(k, 2)
                dve.wait_ge(y_done, upto(8 * K + k + 1, i, 8))
                part = x[:, t, half * HALF:(half + 1) * HALF]
                dve.scalar_tensor_tensor(out=part, in0=banks[k % len(banks)][:], scalar=weight / ALPHA, in1=part,
                                         op0=ALU.mult, op1=ALU.add).then_inc(y_added, 1)

            chain = [0]

            def then(op):
                op.then_inc(stat_done, 1)
                chain[0] += 1
                dve.wait_ge(stat_done, chain[0])

            def logits(u):
                head, tiles, col, _ = attention_unit(u)
                width = sum(len(keys) for _, keys in tiles) * P
                table = dist_swa if u < 8 else dist_moba[u % 2]
                dve.wait_ge(scores_done, u + 1)
                if u >= 3:
                    dve.wait_ge(probs_turned, u - 2)
                lg = probs[:, u % 3, 0:width]
                dve.scalar_tensor_tensor(out=lg, in0=table, scalar=-SLOPES[head],
                                         in1=psum[:, 2 * T + col:2 * T + col + width],
                                         op0=ALU.mult, op1=ALU.add).then_inc(scores_kept, 1)
                dve.wait_ge(scores_kept, u + 1)
                at = 0
                for n_, (tile, keys) in enumerate(tiles):
                    op = dve.tensor_reduce(neg_max[:, u % 3, n_:n_ + 1], probs[:, u % 3, at:at + len(keys) * P],
                                           AX.X, ALU.max, negate=True)
                    at += len(keys) * P
                if head < 8:
                    op.then_inc(max_ready, 1)
                    dve.wait_ge(max_ready, u + 1)
                    op = dve.tensor_scalar(neg_max[:, u % 3, :], neg_max[:, u % 3, :], neg_sink[:, head:head + 1],
                                           None, ALU.min)
                op.then_inc(neg_max_ready, 1)

            def probs_second_bank(u):
                blocks = sum(len(keys) for _, keys in attention_unit(u)[1])
                if blocks > 4:
                    dve.wait_ge(probs_turned, u + 1)
                    dve.tensor_copy(probs_t[:, u % 2, 4 * P:blocks * P],
                                    bank[5][:, 0:(blocks - 4) * P]).then_inc(probs_t_dve, 1)

            def keep_head(u):
                head, _, _, ends = attention_unit(u)
                if not ends:
                    return
                dve.wait_ge(head_done, head + 1)
                dve.wait_ge(exp_done, u + 1)
                sum_ = sums[:, head % 4, :]
                if head < 8:
                    then(dve.tensor_tensor(total[:], sum_, sink_part[:, head % 4, :], ALU.add))
                    sum_ = total[:]
                then(dve.reciprocal(inv_sum[:], sum_))
                dve.tensor_tensor(att_out[head // 4 % 2][:, :, (head % 4) * HD:(head % 4 + 1) * HD],
                                  bank[6 + head % 2][:, 0:NT * HD].rearrange("p (t n) -> p t n", n=HD),
                                  inv_sum[:, :, None].broadcast_to([P, NT, HD]), ALU.mult).then_inc(head_kept, 1)

            def decays_and_keys(g, j, first_block):
                head = 2 * g + j
                dve.wait_ge(proj_kept, first_block + blocks_until("hgrn", "f", g) - 1 + j)
                dve.tensor_scalar(decay[:, g % 2, j, :], sig_pos[:, j, :], span[:, head:head + 1],
                                  lower[:, head:head + 1], ALU.mult, ALU.add)
                dve.tensor_scalar(ks[:, g % 2, j, :], sig_neg[:, j, :], span[:, head:head + 1], None,
                                  ALU.mult).then_inc(keys_ready, 1)

            def level(g, a):
                q_, k_, par = qp[:, g % 2], ks[:, g % 2], g % 2
                dve.wait_ge(level_done, 8 * g + a + 1)
                if a == 0:
                    for h in range(2):
                        dve.tensor_tensor(within[:, h, :].rearrange("p (c t) -> p c t", t=P),
                                          bank[2 + h].rearrange("p (c t) -> p c t", t=P),
                                          ident[:, None, :].broadcast_to([P, 4, P]), ALU.mult)
                    dve.tensor_tensor(q_, q_, decay[:, par], ALU.mult).then_inc(level_kept, 1)
                    dve.wait_ge(level_kept, 8 * g + 1)
                    return
                m = LEVELS[a - 1]
                n_ = T // (2 * m)
                pairs = "p h (b two e) -> p (h b) two e"
                at = within[:].rearrange(pairs, two=2, e=m)[:, :, 1, :]
                dst = at.rearrange("p (x b) e -> p x b e", b=64 // m)
                dve.copy_predicated(dst, pair_mask[:, a - 1, :].rearrange("p (b e) -> p b e", e=m)[:, None, :, :]
                                    .broadcast_to([P, 8, 64 // m, m]),
                                    bank[2 + a % 2].rearrange("p (x b e) -> p x b e", b=64 // m, e=m))
                old = decay[:, par].rearrange("p h t -> p (h t)") if m == 1 else \
                    block_decay[:, decay_at(m):decay_at(m) + 2 * T // m]
                old = old.rearrange("p (b two) -> p b two", two=2)
                qv = q_.rearrange(pairs, two=2, e=m)[:, :, 1, :]
                kv = k_.rearrange(pairs, two=2, e=m)[:, :, 0, :]
                dve.tensor_tensor(qv, qv, old[:, :, 0:1].broadcast_to([P, 2 * n_, m]), ALU.mult)
                dve.tensor_tensor(kv, kv, old[:, :, 1:2].broadcast_to([P, 2 * n_, m]), ALU.mult)
                dve.tensor_tensor(block_decay[:, decay_at(2 * m):decay_at(2 * m) + 2 * n_], old[:, :, 0],
                                  old[:, :, 1], ALU.mult).then_inc(level_kept, 1)
                dve.wait_ge(level_kept, 8 * g + a + 1)

            def states(g):
                dve.wait_ge(updates_done, g + 1)
                for c in range(3):
                    for h in range(2):
                        upd = bank[2 + h][:, c * P:(c + 1) * P]
                        if c == 0:
                            op = dve.tensor_copy(state[:, h, 0, :], upd)
                        else:
                            whole = block_decay[:, decay_at(P) + 4 * h + c:decay_at(P) + 4 * h + c + 1]
                            op = dve.scalar_tensor_tensor(out=state[:, h, c, :], in0=state[:, h, c - 1, :],
                                                          scalar=whole, in1=upd, op0=ALU.mult, op1=ALU.add)
                    if c < 2:
                        then(op)
                op.then_inc(states_ready, 1)

            def mean_squares(g):
                dve.wait_ge(squares_done, 2 * g + 2)
                then(dve.tensor_reduce(mean_sq[:], squares, AX.X, ALU.add))
                dve.tensor_scalar(rms_in[:], mean_sq[:], 1.0 / P, RMS_EPS, ALU.mult, ALU.add).then_inc(rms_asked, 1)

            def norm_outputs(g):
                dve.wait_ge(rms_ready, g + 1)
                dve.wait_ge(gate_normed, g + 1)
                dve.wait_ge(keys_tok_ready, 2 * g + 2)
                for t in range(NT):
                    for h in range(2):
                        op = dve.scalar_tensor_tensor(
                            out=normed[:, t, h * P:(h + 1) * P],
                            in0=bank[4 + t // 2][:, (t % 2) * GW + h * P:(t % 2) * GW + (h + 1) * P],
                            scalar=rms[:, 2 * t + h:2 * t + h + 1], in1=out_gate[:, g % 2, t, h * P:(h + 1) * P],
                            op0=ALU.mult, op1=ALU.mult)
                op.then_inc(normed_ready, 1)

            def last_down_and_norm(n, K, weight):
                def add_pieces(t):
                    for k in (2 * t, 2 * t + 1):
                        add_piece(K, k, weight, LAST_BANKS)

                def moments(t):
                    dve.wait_ge(y_added, FREE_AT_START + 8 * K + 2 * t + 1)
                    dve.bn_stats(stats[:, 0, :], x[:, t, 0:HALF])
                    dve.wait_ge(y_added, FREE_AT_START + 8 * K + 2 * t + 2)
                    then(dve.bn_stats(stats[:, 1, :], x[:, t, HALF:D]))
                    then(dve.bn_aggr(meanvar[:, t, :], stats[:, :, :]))
                    dve.tensor_scalar(vareps[:, t:t + 1], meanvar[:, t, 1:2], LN_EPS, None,
                                      ALU.add).then_inc(var_ready, 1)

                def normalise(t):
                    if t == 0:
                        dve.wait_ge(par_loaded[0], 16 * (n + 1))
                        dve.wait_ge(par_loaded[1], 16 * (n + 1))
                    dve.scalar_tensor_tensor(out=x[:, t, :], in0=x[:, t, :], scalar=meanvar[:, t, 0:1],
                                             in1=lng[:], op0=ALU.subtract, op1=ALU.mult).then_inc(centred, 1)
                    dve.wait_ge(centred, NT * n + t + 1)
                    dve.wait_ge(rstd_ready, NT * n + t + 1)
                    dve.scalar_tensor_tensor(out=x[:, t, :], in0=x[:, t, :], scalar=rstd[:, t:t + 1],
                                             in1=lnb[:], op0=ALU.mult, op1=ALU.add).then_inc(ln_done, 1)

                def low_(t):
                    if n < last_phase:
                        turn_low(n + 1, t)

                add_pieces(0)
                moments(0)
                add_pieces(1)
                moments(1)
                normalise(0)
                normalise(1)
                if phases[n][0] != "ffn":
                    add_pieces(2)
                low_(0)
                low_(1)
                if phases[n][0] == "ffn":
                    add_pieces(2)
                moments(2)
                add_pieces(3)
                moments(3)
                normalise(2)
                normalise(3)
                low_(2)
                low_(3)

            def first_low(s):
                dve.wait_ge(hi_ready, s + 1)
                dve.tensor_tensor(w_lo[:, s, :], raw[:, s, :], w_hi[:, s, :].bitcast(F32),
                                  ALU.subtract).then_inc(lo_ready, 1)

            turn_low(0, 0)
            first_low(0)
            turn_low(0, 1)
            first_low(1)
            turn_low(0, 2)
            turn_low(0, 3)
            dve.wait_ge(lb_exp, 1)
            dve.memset(stats[:], 0.0).then_inc(y_added, FREE_AT_START)
            dve.tensor_tensor(lb_m[:], lb_t[:, 0, :], lb_t[:, 1, :], ALU.max).then_inc(set_up, 1)
            dve.wait_ge(set_up, 1)
            dve.tensor_tensor(lb_t[:], lb_t[:], lb_m[:, None, :].broadcast_to([P, 2, 8]),
                              ALU.subtract).then_inc(set_up, 1)
            dve.wait_ge(lb_exp, 2)
            dve.tensor_tensor(lb_m[:], lb_e[:, 0, :], lb_e[:, 1, :], ALU.add).then_inc(set_up, 1)
            dve.wait_ge(set_up, 3)
            dve.reciprocal(lb_r[:], lb_m[:]).then_inc(set_up, 1)
            dve.wait_ge(set_up, 4)
            dve.tensor_tensor(lower[:], lb_e[:, 1, :], lb_r[:], ALU.mult)
            dve.tensor_tensor(span[:], lb_e[:, 0, :], lb_r[:], ALU.mult)
            dve.wait_ge(small_loaded, 48)
            dve.tensor_scalar(neg_sink[:], sink_b[:], -1.0, None, ALU.mult)
            dve.wait_ge(masks_step, MASK_STEPS)
            dve.tensor_copy(pair_mask[:], pair_mask_f).then_inc(set_up, 1)
            dve.wait_ge(set_up, 5)
            for n, (kind, _, _, weight) in enumerate(phases):
                s0, K0, H0 = bases[n]
                if kind == "ffn":
                    G0 = NG * ffn_index[n]
                    hiddens(G0)
                    hid_low(H0)
                    with dve.Fori(0, NG - 2) as i:
                        for k in range(8):
                            add_piece(K0, k, weight, bank[4:8], i)
                        hiddens(G0 + 1, i)
                        hid_low(H0 + 1, i)
                    dve.wait_ge(h_lo_done, 2 * (H0 + NG - 1))
                    hiddens(G0 + NG - 1)
                    for j in range(2):
                        dve.wait_ge(h_hi_done, 2 * (H0 + NG - 1) + j + 1)
                        dve.tensor_tensor(last_h(xt_lo, j), hid[:, j, :].rearrange("p (c n) -> p c n", c=2),
                                          last_h(xt_hi, j).bitcast(F32), ALU.subtract).then_inc(h_lo_done, 1)
                    last_down_and_norm(n, K0 + NG - 2, weight)
                else:
                    slabs, plan = mixer_slabs(kind), mixer_schedule(kind)
                    banks = bank[0:2] if kind == "attn" else bank[6:8]
                    outs = out_base[n]
                    if kind == "attn":
                        dve.wait_ge(masks_step, MASK_STEPS + TABLE_STEPS)
                    if kind == "hgrn":
                        decays_and_keys(0, 0, block_base[n])
                        decays_and_keys(0, 1, block_base[n])
                    for step in plan:
                        if step[0] == "quarter":
                            name, g = slabs[step[1]]
                            if name == "down":
                                add_piece(K0 + g, 2 * step[2], weight, banks)
                                add_piece(K0 + g, 2 * step[2] + 1, weight, banks)
                            if name == "f" and step[2] % 2 == 1:
                                decays_and_keys(g, step[2] // 2, block_base[n])
                        elif step[0] == "scores":
                            logits(step[1])
                        elif step[0] == "turn_probs":
                            probs_second_bank(step[1])
                        elif step[0] == "values":
                            keep_head(step[1])
                        elif step[0] == "level":
                            level(step[1], step[2])
                        elif step[0] == "updates":
                            states(step[1])
                        elif step[0] == "outputs":
                            mean_squares(step[1])
                        elif step[0] == "norm":
                            norm_outputs(step[1])
                        elif step[0] == "turn_out":
                            for j in range(2):
                                dve.wait_ge(h_hi_done, 2 * (H0 + step[1]) + j + 1)
                                src, high_, low_ = bank[4 + j], h_hi[:, j, :], h_lo[:, j, :]
                                if step[1] == 3:
                                    src, high_, low_ = (src.rearrange("p (c n) -> p c n", c=2), last_h(xt_hi, j),
                                                        last_h(xt_lo, j))
                                dve.tensor_tensor(low_, src, high_.bitcast(F32), ALU.subtract).then_inc(h_lo_done, 1)
                    last_down_and_norm(n, K0 + 3, weight)

        @block.tensor
        def _(pe):
            def three(out_, w, xs, first, last):
                pe.matmul(out_, w[0], xs[0], start=first, stop=False)
                pe.matmul(out_, w[0], xs[1], start=False, stop=False)
                return pe.matmul(out_, w[1], xs[0], start=False, stop=last)

            def features(out_, slot, j, tok):
                for c in range(DC):
                    cols = slice(c * GW + j * P, c * GW + (j + 1) * P)
                    mm = three(out_, (w_hi[:, slot, cols], w_lo[:, slot, cols]),
                               (xt_hi[:, c, tok], xt_lo[:, c, tok]), c == 0, c == DC - 1)
                return mm

            def turn(turn_no, t):
                if t >= 2:
                    pe.wait_ge(xt_lo_done, 8 * turn_no + 2 * (t - 1))
                if turn_no:
                    pe.wait_ge(ln_done, NT * (turn_no - 1) + t + 1)
                else:
                    pe.wait_ge(x_loaded[t], 16)
                for b in range(2):
                    for c in range(4):
                        mm = pe.transpose(bank[4 + 2 * (t % 2) + b][:, c * P:(c + 1) * P],
                                          x[:, t, (4 * b + c) * P:(4 * b + c + 1) * P], ident[:])
                    mm.then_inc(turn_done, 1)

            def up(s, G, done, freed, b0, i=None):
                pe.wait_ge(lo_ready, upto(s + 1, i, RING))
                for j in range(2):
                    pe.wait_ge(freed, upto(2 * G - 1 + j, i, 2))
                    features(bank[b0 + j], s % RING, j, slice(0, T)).then_inc(done, 1)

            def begin(n, first_two):
                K = bases[n][1]
                if n == 0 or phases[n - 1][0] != "ffn":
                    turn(n, 0)
                    turn(n, 1)
                pe.wait_ge(lo_ready, bases[n][0] + 1)
                if n:
                    pe.wait_ge(y_added, FREE_AT_START + 8 * K - 2)
                pe.wait_ge(xt_lo_done, 8 * n + 4)
                first_two(0, 0, (0, 1))
                pe.wait_ge(lo_ready, bases[n][0] + 2)
                if n:
                    pe.wait_ge(y_added, FREE_AT_START + 8 * K)
                first_two(1, 0, (0,))
                turn(n, 2)
                turn(n, 3)
                first_two(1, 0, (1,))
                pe.wait_ge(xt_lo_done, 8 * n + 8)
                first_two(0, 1, (0, 1))
                if n == 0:
                    pe.wait_ge(small_loaded, 48)
                    pe.transpose(bank[4][:, 0:16], lb_rows[:], ident[0:16, 0:16]).then_inc(lb_turned, 1)
                first_two(1, 1, (0, 1))

            def down(s, K, H, i=None):
                for t in range(NT):
                    down_quarter(s, K, H, t, bank[4:8], i)

            def left_operand(c, t, last):
                if last:
                    in_half = slice(t % 2 * P, t % 2 * P + P)
                    return last_h(xt_hi, c)[:, t // 2, in_half], last_h(xt_lo, c)[:, t // 2, in_half]
                return h_hi[:, c, t * P:(t + 1) * P], h_lo[:, c, t * P:(t + 1) * P]

            def down_quarter(s, K, H, t, banks, i=None, last=False):
                slot = s % RING
                if t == 0:
                    pe.wait_ge(lo_ready, upto(s + 1, i, RING))
                    pe.wait_ge(h_lo_done, upto(2 * H + 2, i, 2))
                for k in (2 * t, 2 * t + 1):
                    half = k % 2
                    if len(banks) <= 4 or k < 4:
                        pe.wait_ge(y_added, upto(8 * K + k + 1 + FREE_AT_START - min(len(banks), 4), i, 8))
                    for c in range(2):
                        cols = slice(c * D + half * HALF, c * D + (half + 1) * HALF)
                        mm = three(banks[k % len(banks)][:], left_operand(c, t, last),
                                   (w_hi[:, slot, cols], w_lo[:, slot, cols]), c == 0, c == 1)
                    mm.then_inc(y_done, 1)

            def last_downs(n, s, K, H):
                def part(which, tiles):
                    slot = (s + which) % RING
                    for t in tiles:
                        for half in range(2):
                            for c in range(2):
                                cols = slice(c * D + half * HALF, c * D + (half + 1) * HALF)
                                mm = three(LAST_BANKS[2 * t + half][:], left_operand(c, t, which == 1),
                                           (w_hi[:, slot, cols], w_lo[:, slot, cols]),
                                           which == 0 and c == 0, which == 1 and c == 1)
                            if which:
                                mm.then_inc(y_done, 1)
                    return mm

                pe.wait_ge(lo_ready, s + 1)
                pe.wait_ge(h_lo_done, 2 * H)
                pe.wait_ge(y_added, FREE_AT_START + 8 * K)
                part(0, (0, 1))
                pe.wait_ge(lo_ready, s + 2)
                pe.wait_ge(h_lo_done, 2 * H + 2)
                part(1, (0, 1))
                part(0, (2, 3)).then_inc(first_down_of_two, 1)
                if n < last_phase:
                    turn(n + 1, 0)
                part(1, (2,))
                if n < last_phase:
                    turn(n + 1, 1)
                part(1, (3,))

            def token_tiles(out_, slot, tiles, n_, first_col):
                for t in tiles:
                    at = t * n_ % T
                    tok = slice(t * P, (t + 1) * P)
                    for c in range(DC):
                        cols = slice(c * GW + first_col, c * GW + first_col + n_)
                        mm = three(out_[:, at:at + n_], (xt_hi[:, c, tok], xt_lo[:, c, tok]),
                                   (w_hi[:, slot, cols], w_lo[:, slot, cols]), c == 0, c == DC - 1)
                return mm

            def mixer_first_two(s0, slabs):
                def first_two(s, half, tiles):
                    for j in tiles:
                        out_ = bank[proj_bank(s, j)]
                        if slabs[s][0] == "kv" and j == 1:
                            mm = token_tiles(out_, (s0 + s) % RING, [2 * half, 2 * half + 1], P, P)
                        else:
                            tok = slice(half * T // 2, (half + 1) * T // 2)
                            mm = features(out_[:, tok], (s0 + s) % RING, j, tok)
                        if half:
                            mm.then_inc(proj_done, 1)
                return first_two

            def ffn_first_two(s0):
                def first_two(s, half, tiles):
                    tok = slice(half * T // 2, (half + 1) * T // 2)
                    for j in tiles:
                        mm = features(bank[2 * s + j][:, tok], (s0 + s) % RING, j, tok)
                        if half:
                            mm.then_inc((up1_done, up3_done)[s], 1)
                return first_two

            def projected(s, name, quarter, block):
                slot = s % RING
                j, half = divmod(quarter, 2)
                if quarter == 0:
                    pe.wait_ge(lo_ready, s + 1)
                if half == 0:
                    pe.wait_ge(proj_kept, block - 1)
                out_ = bank[j]
                token_major = name in ("v", "g", "vb")
                if not token_major:
                    for c in range(4 * half, 4 * half + 4):
                        cols = slice(c * GW + j * P, c * GW + (j + 1) * P)
                        mm = three(out_, (w_hi[:, slot, cols], w_lo[:, slot, cols]),
                                   (xt_hi[:, c, :], xt_lo[:, c, :]), c == 0, c == DC - 1)
                else:
                    mm = token_tiles(out_, slot, [2 * j + half], GW, 0)
                if half == 1:
                    mm.then_inc(proj_done, 1)

            def scores(u, blocks_needed):
                head, tiles, col, _ = attention_unit(u)
                g = head // 4
                rows = slice((head % 2) * HD, (head % 2 + 1) * HD)
                if u:
                    pe.wait_ge(scores_kept, u)
                pe.wait_ge(proj_kept, blocks_needed)
                if u == 0:
                    pe.wait_ge(kv_copied[0], 16)
                    pe.wait_ge(kv_copied[1], 16)
                at = 2 * T + col
                for tile, keys in tiles:
                    kt = k_swa[rows, g, :] if head < 8 else k_moba[rows, g % 2, (head % 4) // 2, :]
                    mm = pe.matmul(psum[:, at:at + len(keys) * P],
                                   q_t[rows, g % 2, (head % 4) // 2, tile * P:(tile + 1) * P],
                                   kt[:, keys[0] * P:(keys[-1] + 1) * P], start=True, stop=True)
                    at += len(keys) * P
                mm.then_inc(scores_done, 1)

            def turn_probs(u, H):
                blocks = sum(len(keys) for _, keys in attention_unit(u)[1])
                pe.wait_ge(exp_done, u + 1)
                if u:
                    pe.wait_ge(probs_t_act, u)
                    pe.wait_ge(probs_t_dve, two_bank_units(u))
                if H:
                    pe.wait_ge(h_lo_done, 2 * H)
                for b in range(blocks):
                    mm = pe.transpose(psum[:, 4 * T + b * P:4 * T + (b + 1) * P],
                                      probs[:, u % 3, b * P:(b + 1) * P], ident[:])
                mm.then_inc(probs_turned, 1)

            def weigh_values(u, blocks_needed):
                head, tiles, _, ends = attention_unit(u)
                pe.wait_ge(proj_kept, blocks_needed)
                pe.wait_ge(probs_t_act, u + 1)
                pe.wait_ge(probs_t_dve, two_bank_units(u + 1))
                if head >= 2:
                    pe.wait_ge(head_kept, head - 1)
                b = 0
                for tile, keys in tiles:
                    for key in keys:
                        v_ = v_swa[:, key, (head // 4) * HD:(head // 4 + 1) * HD] if head < 8 else \
                            v_moba[:, (head // 4) % 2, key, (head % 4) * HD:(head % 4 + 1) * HD]
                        mm = pe.matmul(bank[6 + head % 2][:, tile * HD:(tile + 1) * HD],
                                       probs_t[:, u % 2, b * P:(b + 1) * P], v_,
                                       start=key == keys[0], stop=key == keys[-1])
                        b += 1
                if ends:
                    mm.then_inc(head_done, 1)

            def level_products(g, a, blocks_needed):
                if a == 0:
                    pe.wait_ge(proj_kept, blocks_needed)
                    pe.wait_ge(keys_ready, 2 * g + 2)
                    if g:
                        pe.wait_ge(states_ready, g)
                else:
                    pe.wait_ge(level_kept, 8 * g + a)
                for h in range(2):
                    for c in range(4):
                        chunk = slice(c * P, (c + 1) * P)
                        if a == 0:
                            out_, rhs = bank[2 + h][:, chunk], qp[:, g % 2, h, chunk]
                        else:
                            m = LEVELS[a - 1]
                            out_ = bank[2 + a % 2][:, (4 * h + c) * 64:(4 * h + c + 1) * 64]
                            rhs = qp[:, g % 2, h, chunk].rearrange("p (b two e) -> p b two e", two=2, e=m)[:, :, 1, :]
                        mm = pe.matmul(out_, ks[:, g % 2, h, chunk], rhs, start=True, stop=True)
                mm.then_inc(level_done, 1)

            def turn_keys(g, H):
                pe.wait_ge(level_kept, 8 * g + 8)
                if H:
                    pe.wait_ge(h_lo_done, 2 * H)
                for h in range(2):
                    for c in range(4):
                        mm = pe.transpose(bank[4 + h][:, c * P:(c + 1) * P], ks[:, g % 2, h, c * P:(c + 1) * P], ident[:])
                    mm.then_inc(keys_turned, 1)

            def updates(g, blocks_needed):
                pe.wait_ge(keys_tok_ready, 2 * g + 2)
                pe.wait_ge(proj_kept, blocks_needed)
                for h in range(2):
                    for c in range(3):
                        mm = pe.matmul(bank[2 + h][:, c * P:(c + 1) * P], keys_tok[:, h, c * P:(c + 1) * P],
                                       values[:, g % 2, c, h * P:(h + 1) * P], start=True, stop=True)
                mm.then_inc(updates_done, 1)

            def outputs(g):
                pe.wait_ge(states_ready, g + 1)
                for c in range(4):
                    for h in range(2):
                        out_ = bank[4 + c // 2][:, (c % 2) * GW + h * P:(c % 2) * GW + (h + 1) * P]
                        chunk = slice(c * P, (c + 1) * P)
                        mm = pe.matmul(out_, within[:, h, chunk], values[:, g % 2, c, h * P:(h + 1) * P],
                                       start=True, stop=c == 0)
                        if c:
                            mm = pe.matmul(out_, qp[:, g % 2, h, chunk], state[:, h, c - 1, :], start=False, stop=True)
                    if c % 2:
                        mm.then_inc(outputs_done, 1)

            def turn_out(src):
                for j in range(2):
                    for t in range(NT):
                        mm = pe.transpose(bank[4 + j][:, t * P:(t + 1) * P], src[:, t, j * P:(j + 1) * P], ident[:])
                    mm.then_inc(out_turned, 1)

            pe.wait_ge(consts_ready, 2)
            for n, (kind, _, _, _) in enumerate(phases):
                s0, K0, H0 = bases[n]
                if kind == "ffn":
                    G0 = NG * ffn_index[n]
                    begin(n, ffn_first_two(s0))
                    with pe.Fori(0, NG - 2) as i:
                        up(s0 + 2, G0 + 1, up1_done, gate_done, 0, i)
                        down(s0 + 3, K0, H0, i)
                        up(s0 + 4, G0 + 1, up3_done, hid_done, 2, i)
                    up(s0 + 3 * NG - 4, G0 + NG - 1, up1_done, gate_done, 0)
                    up(s0 + 3 * NG - 3, G0 + NG - 1, up3_done, hid_done, 2)
                    last_downs(n, s0 + 3 * NG - 2, K0 + NG - 2, H0 + NG - 1)
                else:
                    slabs, plan = mixer_slabs(kind), mixer_schedule(kind)
                    banks = bank[0:2] if kind == "attn" else bank[6:8]
                    first = block_base[n]
                    block = first + 4
                    turned = outs = 0
                    begin(n, mixer_first_two(s0, slabs))
                    for step in plan:
                        what, g = step[0], step[1]
                        if what == "quarter":
                            name, group = slabs[step[1]]
                            if name == "down":
                                if step[2] == 0 and kind == "attn":
                                    pe.wait_ge(proj_kept, block)
                                down_quarter(s0 + step[1], K0 + group, H0 + group, step[2], banks)
                            else:
                                if kind == "attn" and step[2] == 0:
                                    downs = sum(x[0] == "down" for x in slabs[:step[1]])
                                    pe.wait_ge(y_added, 8 * (K0 + downs) + FREE_AT_START)
                                projected(s0 + step[1], name, step[2], block)
                                block += step[2] % 2
                        elif what == "scores":
                            group = attention_unit(step[1])[0] // 4
                            scores(step[1], first + blocks_until(kind, "q", group))
                        elif what == "turn_probs":
                            turn_probs(step[1], H0 + outs)
                            turned = step[1] + 1
                        elif what == "values":
                            group = attention_unit(step[1])[0] // 4
                            weigh_values(step[1], first + (blocks_until(kind, "vb", group) if group > 1 else 2))
                        elif what == "level":
                            level_products(g, step[2], first + blocks_until(kind, "q", g))
                        elif what == "turn_keys":
                            turn_keys(g, H0 + g)
                        elif what == "updates":
                            updates(g, first + blocks_until(kind, "v", g))
                        elif what == "outputs":
                            outputs(g)
                        elif what == "norm":
                            pass
                        elif kind == "attn":
                            pe.wait_ge(head_kept, 4 * g + 4)
                            pe.wait_ge(probs_t_act, turned)
                            pe.wait_ge(probs_t_dve, two_bank_units(turned))
                            turn_out(att_out[g % 2])
                            outs += 1
                        else:
                            pe.wait_ge(normed_ready, g + 1)
                            turn_out(normed)
                    for t in range(NT):
                        down_quarter(s0 + len(slabs) - 1, K0 + 3, H0 + 3, t, LAST_BANKS, last=True)


_INS = ["x", "ffn_w1", "ffn_w3", "ffn_w2", "ln_g", "ln_b", "attn_w_in", "attn_sinks", "attn_w_out",
        "hgrn_w_in", "hgrn_norm_g", "hgrn_w_out", "hgrn_lower_bounds"]


def kernel(**inputs):
    import concourse.bacc as bacc
    from concourse.bass_utils import run_bass_kernel_spmd

    nc = bacc.Bacc("TRN2", target_bir_lowering=False, num_devices=1)
    arrays, args = {}, []
    for name in _INS:
        a = np.ascontiguousarray(inputs[name])
        arrays[f"in_{name}"] = a
        args.append(nc.dram_tensor(f"in_{name}", a.shape, mybir.dt.from_np(a.dtype), kind="ExternalInput").ap())
    args.append(nc.dram_tensor("out_x", (1, T, D), F32, kind="ExternalOutput").ap())
    build_trunk(nc, *args)
    return run_bass_kernel_spmd(nc, [arrays], core_ids=[0]).results[0]["out_x"]
```
